# Optimizing a Trainium2 kernel written in Bass

```python
import jax, jax.numpy as jnp
from jax import lax
import numpy as np

D_MODEL = 1024
BATCH = 1
SEQ = 512
DEPTH = 2

N_META = 16
FOX_HEADS = 16
FOX_HEAD_DIM = D_MODEL // FOX_HEADS
Q_BLOCK = 128
HGRN_EXPAND = 128
HGRN_HEADS = D_MODEL // HGRN_EXPAND
HGRN_CHUNK = 64
D_FF = ((8 * D_MODEL // 3 + 127) // 128) * 128
CONV_WIDTH = 3
EPS = 1e-6
N_FOX_LAYERS = (DEPTH + 1) // 2
N_HGRN_LAYERS = DEPTH // 2


def rms_norm(x, gain):
    x32 = x.astype(jnp.float32)
    y = x32 * lax.rsqrt(jnp.mean(x32 * x32, axis=-1, keepdims=True) + EPS)
    return (y * gain.astype(jnp.float32)).astype(x.dtype)

def fox_attention(h, norm_g, w_in, b_f, q_gain, k_gain, w_out):
    B, L, D = h.shape
    H, hd = FOX_HEADS, FOX_HEAD_DIM
    xn = rms_norm(h, norm_g)
    q, k, v, f_logit, o_gate = jnp.split(xn @ w_in, [D, 2 * D, 3 * D, 3 * D + H], axis=-1)
    q = rms_norm(q.reshape(B, L, H, hd), q_gain).astype(jnp.float32) * (hd ** -0.5)
    k = rms_norm(k.reshape(B, L, H, hd), k_gain).astype(jnp.float32)
    v = v.reshape(B, L, H, hd)
    log_f = jax.nn.log_sigmoid((f_logit + b_f).astype(jnp.float32))
    c = jnp.cumsum(log_f, axis=1).transpose(0, 2, 1)
    key_pos = jnp.arange(L)

    def attend(q_blk, c_blk, q_pos):
        s = jnp.einsum('bqhd,bkhd->bhqk', q_blk, k)
        s = s + c_blk[..., None] - c[:, :, None, :]
        s = jnp.where(q_pos[:, None] >= key_pos[None, :], s, -jnp.inf)
        p = jax.nn.softmax(s, axis=-1)
        return jnp.einsum('bhqk,bkhd->bqhd', p.astype(v.dtype), v)

    o_meta = attend(q[:, :N_META], c[:, :, :N_META], jnp.arange(N_META))
    n_blk = (L - N_META) // Q_BLOCK
    q_r = q[:, N_META:].reshape(B, n_blk, Q_BLOCK, H, hd).transpose(1, 0, 2, 3, 4)
    c_r = c[:, :, N_META:].reshape(B, H, n_blk, Q_BLOCK).transpose(2, 0, 1, 3)
    pos_r = (N_META + jnp.arange(L - N_META)).reshape(n_blk, Q_BLOCK)
    o_r = lax.map(lambda a: attend(*a), (q_r, c_r, pos_r))
    o_r = o_r.transpose(1, 0, 2, 3, 4).reshape(B, L - N_META, H, hd)
    o = jnp.concatenate([o_meta, o_r], axis=1).reshape(B, L, D)
    o = o * jax.nn.sigmoid(o_gate)
    return o @ w_out

def hgrn2_chunk(S, q, k, v, log_f):
    C = q.shape[2]
    b = jnp.cumsum(log_f, axis=2)
    causal = jnp.arange(C)[:, None] >= jnp.arange(C)[None, :]
    diff = b[:, :, :, None, :] - b[:, :, None, :, :]
    decay = jnp.exp(jnp.where(causal[None, None, :, :, None], diff, -jnp.inf))
    scores = jnp.einsum('bhtk,bhtsk,bhsk->bhts', q, decay, k)
    o = jnp.einsum('bhts,bhsv->bhtv', scores, v) + jnp.einsum('bhtk,bhkv->bhtv', q * jnp.exp(b), S)
    b_end = b[:, :, -1]
    S_new = jnp.exp(b_end)[..., None] * S + jnp.einsum(
        'bhsk,bhsv->bhkv', k * jnp.exp(b_end[:, :, None, :] - b), v)
    return S_new, o

def hgrn2_mixer(h, norm_g, w_in, lower_bound, o_gain, w_out):
    B, L, D = h.shape
    H, dk = HGRN_HEADS, HGRN_EXPAND
    xn = rms_norm(h, norm_g)
    q, f_logit, i, g = jnp.split(xn @ w_in, 4, axis=-1)
    lb = lower_bound.astype(jnp.float32)
    f = lb + (1.0 - lb) * jax.nn.sigmoid(f_logit.astype(jnp.float32))

    def to_heads(t):
        return t.astype(jnp.float32).reshape(B, L, H, dk).transpose(0, 2, 1, 3)

    q = to_heads(jax.nn.silu(q))
    k = to_heads(1.0 - f)
    log_f = to_heads(jnp.log(f))
    v = to_heads(i)
    S0 = jnp.zeros((B, H, dk, dk), jnp.float32)
    S, o_meta = hgrn2_chunk(S0, q[:, :, :N_META], k[:, :, :N_META], v[:, :, :N_META], log_f[:, :, :N_META])
    n_chunk = (L - N_META) // HGRN_CHUNK

    def chunks(t):
        return t[:, :, N_META:].reshape(B, H, n_chunk, HGRN_CHUNK, dk).transpose(2, 0, 1, 3, 4)

    _, o_r = lax.scan(lambda s, a: hgrn2_chunk(s, *a), S, (chunks(q), chunks(k), chunks(v), chunks(log_f)))
    o_r = o_r.transpose(1, 2, 0, 3, 4).reshape(B, H, L - N_META, dk)
    o = jnp.concatenate([o_meta, o_r], axis=2).transpose(0, 2, 1, 3)
    o = rms_norm(o, o_gain).reshape(B, L, D) * jax.nn.sigmoid(g.astype(jnp.float32))
    return o.astype(h.dtype) @ w_out

def conv_ffn(h, norm_g, w_gate, w_up, conv_w, conv_b, w_down):
    xn = rms_norm(h, norm_g)
    a = xn @ w_gate
    L = a.shape[1]
    a_pad = jnp.pad(a, ((0, 0), (CONV_WIDTH - 1, 0), (0, 0)))
    a = (conv_b + conv_w[0] * a_pad[:, 0:L] + conv_w[1] * a_pad[:, 1:L + 1]
         + conv_w[2] * a_pad[:, 2:L + 2])
    return (jax.nn.silu(a) * (xn @ w_up)) @ w_down

def first_inputs(seed: int = 0) -> dict:
    key = jax.random.key(seed)
    ks = jax.random.split(key, 19)
    D, F, H = D_MODEL, D_FF, FOX_HEADS
    nF, nH = N_FOX_LAYERS, N_HGRN_LAYERS

    def normal(k, shape, scale):
        return scale * jax.random.normal(k, shape, jnp.float32)

    def gain(k, shape):
        return 1.0 + normal(k, shape, 0.05)

    return {
        "x": normal(ks[0], (BATCH, SEQ, D), 1.0),
        "meta_tokens": normal(ks[1], (N_META, D), 1.0),
        "fox_norm": gain(ks[2], (nF, D)),
        "fox_w_in": normal(ks[3], (nF, D, 4 * D + H), D ** -0.5),
        "fox_b_f": 2.0 + normal(ks[4], (nF, H), 0.1),
        "fox_q_gain": gain(ks[5], (nF, FOX_HEAD_DIM)),
        "fox_k_gain": gain(ks[6], (nF, FOX_HEAD_DIM)),
        "fox_w_out": normal(ks[7], (nF, D, D), D ** -0.5),
        "hgrn_norm": gain(ks[8], (nH, D)),
        "hgrn_w_in": normal(ks[9], (nH, D, 4 * D), D ** -0.5),
        "hgrn_lower_bounds": normal(ks[10], (DEPTH, D), 0.1),
        "hgrn_o_gain": gain(ks[11], (nH, HGRN_EXPAND)),
        "hgrn_w_out": normal(ks[12], (nH, D, D), D ** -0.5),
        "ffn_norm": gain(ks[13], (DEPTH, D)),
        "ffn_w_gate": normal(ks[14], (DEPTH, D, F), D ** -0.5),
        "ffn_w_up": normal(ks[15], (DEPTH, D, F), D ** -0.5),
        "ffn_conv_w": normal(ks[16], (DEPTH, CONV_WIDTH, F), CONV_WIDTH ** -0.5),
        "ffn_conv_b": normal(ks[17], (DEPTH, F), 0.02),
        "ffn_w_down": normal(ks[18], (DEPTH, F, D), F ** -0.5),
    }

def first_block(x, meta_tokens, fox_norm, fox_w_in, fox_b_f, fox_q_gain, fox_k_gain, fox_w_out,
              hgrn_norm, hgrn_w_in, hgrn_lower_bounds, hgrn_o_gain, hgrn_w_out,
              ffn_norm, ffn_w_gate, ffn_w_up, ffn_conv_w, ffn_conv_b, ffn_w_down):
    B = x.shape[0]
    meta = jnp.broadcast_to(meta_tokens[None].astype(x.dtype), (B, N_META, D_MODEL))
    h = jnp.concatenate([meta, x], axis=1)
    p_lb = jax.nn.softmax(hgrn_lower_bounds.astype(jnp.float32), axis=0)
    lower_bounds = jnp.cumsum(p_lb, axis=0) - p_lb[0]
    for layer in range(DEPTH):
        j = layer // 2
        if layer % 2 == 0:
            h = h + fox_attention(h, fox_norm[j], fox_w_in[j], fox_b_f[j], fox_q_gain[j],
                                  fox_k_gain[j], fox_w_out[j])
        else:
            h = h + hgrn2_mixer(h, hgrn_norm[j], hgrn_w_in[j], lower_bounds[layer],
                                hgrn_o_gain[j], hgrn_w_out[j])
        h = h + conv_ffn(h, ffn_norm[layer], ffn_w_gate[layer], ffn_w_up[layer],
                         ffn_conv_w[layer], ffn_conv_b[layer], ffn_w_down[layer])
    return h[:, N_META:]


DEPTH_2 = 1

CHUNK = 128
PAD = CHUNK - N_META
RET_HEADS = 4
RET_DK = D_MODEL // RET_HEADS
RET_DV = 2 * RET_DK
SB_HEADS = D_MODEL // 64
SB_DH = 64
D_FF_2 = -(-8 * D_MODEL // (3 * 256)) * 256
ROPE_BASE = 10000.0
NORM_EPS = 1e-6
GN_EPS = 1e-5
PROJ_SPLIT = (
    RET_HEADS * RET_DK,
    RET_HEADS * RET_DK,
    RET_HEADS * RET_DV,
    RET_HEADS * RET_DV,
    SB_HEADS * SB_DH,
    SB_HEADS * SB_DH,
    SB_HEADS * SB_DH,
    D_MODEL,
    D_MODEL,
)
PROJ_WIDTH = sum(PROJ_SPLIT)


def rmsnorm(x, g):
    xf = x.astype(jnp.float32)
    y = xf * lax.rsqrt(jnp.mean(xf * xf, axis=-1, keepdims=True) + NORM_EPS)
    return (y * g.astype(jnp.float32)).astype(x.dtype)

def rotary(x, pos):
    half = x.shape[-1] // 2
    inv = ROPE_BASE ** (-jnp.arange(half, dtype=jnp.float32) / half)
    ang = pos[:, None] * inv[None, :]
    cos, sin = jnp.cos(ang), jnp.sin(ang)
    x1, x2 = x[..., :half], x[..., half:]
    return jnp.concatenate([x1 * cos - x2 * sin, x1 * sin + x2 * cos], axis=-1)

def retention_chunkwise(q, k, v):
    B, H, Lp, dk = q.shape
    dv = v.shape[-1]
    n = Lp // CHUNK
    log_g = jnp.log1p(-(2.0 ** (-5.0 - jnp.arange(H, dtype=jnp.float32))))
    idx = jnp.arange(CHUNK, dtype=jnp.float32)
    diff = idx[:, None] - idx[None, :]
    decay = jnp.where(diff >= 0, jnp.exp(log_g[:, None, None] * jnp.maximum(diff, 0.0)), 0.0)
    zeta = jnp.exp(log_g[:, None] * (CHUNK - 1.0 - idx))[:, :, None]
    xi = jnp.exp(log_g[:, None] * (idx + 1.0))[:, :, None]
    g_chunk = jnp.exp(log_g * CHUNK)[:, None, None]

    qc = q.reshape(B, H, n, CHUNK, dk)
    kc = k.reshape(B, H, n, CHUNK, dk)
    vc = v.reshape(B, H, n, CHUNK, dv)
    scores = jnp.einsum('bhncd,bhnsd->bhncs', qc, kc) * decay[:, None]
    inner = jnp.einsum('bhncs,bhnse->bhnce', scores, vc)

    def step(state, inp):
        q_i, k_i, v_i = inp
        cross = jnp.einsum('bhcd,bhde->bhce', q_i, state) * xi
        state = g_chunk * state + jnp.einsum('bhsd,bhse->bhde', k_i, v_i * zeta)
        return state, cross

    s0 = jnp.zeros((B, H, dk, dv), jnp.float32)
    _, cross = lax.scan(step, s0, (qc.transpose(2, 0, 1, 3, 4), kc.transpose(2, 0, 1, 3, 4), vc.transpose(2, 0, 1, 3, 4)))
    out = inner + cross.transpose(1, 2, 0, 3, 4)
    return out.reshape(B, H, Lp, dv)

def head_groupnorm(y):
    mu = jnp.mean(y, axis=-1, keepdims=True)
    var = jnp.mean(jnp.square(y - mu), axis=-1, keepdims=True)
    return (y - mu) * lax.rsqrt(var + GN_EPS)

def stick_breaking(q, k, v):
    Lp, d = q.shape[2], q.shape[3]
    scale = d ** -0.5
    outs = []
    for i in range(Lp // CHUNK):
        lk = (i + 1) * CHUNK
        q_blk = q[:, :, i * CHUNK:lk]
        k_pre, v_pre = k[:, :, :lk], v[:, :, :lk]
        z = jnp.einsum('bhtd,bhsd->bhts', q_blk, k_pre) * scale
        t_pos = i * CHUNK + jnp.arange(CHUNK)
        s_pos = jnp.arange(lk)
        valid = (s_pos[None, :] < t_pos[:, None]) & (s_pos[None, :] >= PAD)
        log_not = jnp.where(valid, jax.nn.log_sigmoid(-z), 0.0)
        after = lax.cumsum(log_not, axis=3, reverse=True) - log_not
        a = jnp.where(valid, jnp.exp(jax.nn.log_sigmoid(z) + after), 0.0)
        outs.append(jnp.einsum('bhts,bhse->bhte', a, v_pre))
    return jnp.concatenate(outs, axis=2)

def hybrid_mixer(hn, w_in, w_ret_out, w_sb_out, w_out):
    B, L, _ = hn.shape
    dtype = hn.dtype
    proj = hn @ w_in
    rq, rk, rv, rg, sq, sk, sv, ga, gb = jnp.split(proj, list(np.cumsum(PROJ_SPLIT)[:-1]), axis=-1)

    def heads(t, h):
        t = t.reshape(B, L, h, -1).transpose(0, 2, 1, 3).astype(jnp.float32)
        return jnp.pad(t, ((0, 0), (0, 0), (PAD, 0), (0, 0)))

    def merge_heads(t):
        t = t[:, :, PAD:]
        return t.transpose(0, 2, 1, 3).reshape(B, L, -1)

    pos = jnp.arange(L + PAD, dtype=jnp.float32) - PAD
    q_r = rotary(heads(rq, RET_HEADS), pos) * (RET_DK ** -0.5)
    k_r = rotary(heads(rk, RET_HEADS), pos)
    y_ret = head_groupnorm(retention_chunkwise(q_r, k_r, heads(rv, RET_HEADS)))
    y_ret = (jax.nn.silu(rg.astype(jnp.float32)) * merge_heads(y_ret)).astype(dtype) @ w_ret_out
    y_sb = merge_heads(stick_breaking(heads(sq, SB_HEADS), heads(sk, SB_HEADS), heads(sv, SB_HEADS)))
    y_sb = y_sb.astype(dtype) @ w_sb_out
    merged = jax.nn.sigmoid(ga) * y_ret + jax.nn.sigmoid(gb) * y_sb
    return merged @ w_out

def swiglu(hn, w_ffn_in, w_ffn_out):
    a, b = jnp.split(hn @ w_ffn_in, 2, axis=-1)
    return (jax.nn.silu(a) * b) @ w_ffn_out

def second_inputs(seed: int = 0) -> dict:
    key = jax.random.key(seed)
    ks = jax.random.split(key, 12)
    f32 = jnp.float32
    nrm = lambda k, shape, fan: jax.random.normal(k, shape, f32) * (fan ** -0.5)
    gain = lambda k: 1.0 + 0.02 * jax.random.normal(k, (DEPTH_2, D_MODEL), f32)
    return {
        "x": jax.random.normal(ks[0], (BATCH, SEQ, D_MODEL), f32),
        "meta_tokens": jax.random.normal(ks[1], (N_META, D_MODEL), f32),
        "w_in": nrm(ks[2], (DEPTH_2, D_MODEL, PROJ_WIDTH), D_MODEL),
        "w_ret_out": nrm(ks[3], (DEPTH_2, RET_HEADS * RET_DV, D_MODEL), RET_HEADS * RET_DV),
        "w_sb_out": nrm(ks[4], (DEPTH_2, SB_HEADS * SB_DH, D_MODEL), SB_HEADS * SB_DH),
        "w_out": nrm(ks[5], (DEPTH_2, D_MODEL, D_MODEL), D_MODEL),
        "w_ffn_in": nrm(ks[6], (DEPTH_2, D_MODEL, 2 * D_FF_2), D_MODEL),
        "w_ffn_out": nrm(ks[7], (DEPTH_2, D_FF_2, D_MODEL), D_FF_2),
        "norm_mix_pre": gain(ks[8]),
        "norm_mix_post": gain(ks[9]),
        "norm_ffn_pre": gain(ks[10]),
        "norm_ffn_post": gain(ks[11]),
    }

def second_block(x, meta_tokens, w_in, w_ret_out, w_sb_out, w_out, w_ffn_in, w_ffn_out,
              norm_mix_pre, norm_mix_post, norm_ffn_pre, norm_ffn_post):
    B = x.shape[0]
    meta = jnp.broadcast_to(meta_tokens.astype(x.dtype)[None], (B, N_META, x.shape[-1]))
    h = jnp.concatenate([meta, x], axis=1)
    for l in range(DEPTH_2):
        mix = hybrid_mixer(rmsnorm(h, norm_mix_pre[l]), w_in[l], w_ret_out[l], w_sb_out[l], w_out[l])
        h = h + rmsnorm(mix, norm_mix_post[l])
        ff = swiglu(rmsnorm(h, norm_ffn_pre[l]), w_ffn_in[l], w_ffn_out[l])
        h = h + rmsnorm(ff, norm_ffn_post[l])
    return h[:, N_META:]


def setup_inputs(seed=0):
    out = dict(first_inputs(seed))
    for name, value in second_inputs(seed + 1).items():
        if name != "x":
            out[name + "_2"] = value
    return out


def reference(
    x, meta_tokens, fox_norm, fox_w_in, fox_b_f, fox_q_gain, fox_k_gain, fox_w_out, hgrn_norm,
    hgrn_w_in, hgrn_lower_bounds, hgrn_o_gain, hgrn_w_out, ffn_norm, ffn_w_gate, ffn_w_up,
    ffn_conv_w, ffn_conv_b, ffn_w_down, meta_tokens_2, w_in_2, w_ret_out_2, w_sb_out_2, w_out_2,
    w_ffn_in_2, w_ffn_out_2, norm_mix_pre_2, norm_mix_post_2, norm_ffn_pre_2, norm_ffn_post_2,
):
    x = first_block(
        x, meta_tokens, fox_norm, fox_w_in, fox_b_f, fox_q_gain, fox_k_gain, fox_w_out,
        hgrn_norm, hgrn_w_in, hgrn_lower_bounds, hgrn_o_gain, hgrn_w_out, ffn_norm, ffn_w_gate,
        ffn_w_up, ffn_conv_w, ffn_conv_b, ffn_w_down,
    )
    return second_block(
        x, meta_tokens_2, w_in_2, w_ret_out_2, w_sb_out_2, w_out_2, w_ffn_in_2, w_ffn_out_2,
        norm_mix_pre_2, norm_mix_post_2, norm_ffn_pre_2, norm_ffn_post_2,
    )


_drawn_inputs = setup_inputs


def setup_inputs(seed=0):
    import zlib

    import numpy as np

    out = dict(_drawn_inputs(seed))
    spreads = {}
    factors = {'fox_b_f': 2.743,
     'fox_q_gain': 3.508,
     'fox_k_gain': 3.481,
     'hgrn_lower_bounds': 6.737,
     'ffn_conv_b': 2.928,
     'norm_mix_post_2': 4.276,
     'norm_ffn_pre_2': 4.019,
     'norm_ffn_post_2': 5.405}
    for name, (base, spread) in spreads.items():
        noise = np.random.default_rng([zlib.crc32(name.encode()), seed]).standard_normal(out[name].shape)
        drawn = base * np.exp(spread * noise) if base else spread * noise
        out[name] = __import__('jax').numpy.asarray(drawn.astype(out[name].dtype))
    for name, factor in factors.items():
        out[name] = (out[name] * factor).astype(out[name].dtype)
    return out
```

```python
from contextlib import ExitStack

import numpy as np

import concourse.bass as bass
from concourse import mybir

F32 = mybir.dt.float32
F32R = mybir.dt.float32r
BF16 = mybir.dt.bfloat16
U8 = mybir.dt.uint8
ALU = mybir.AluOpType
ACT = mybir.ActivationFunctionType
AX = mybir.AxisListType

P = 128
D = 1024
KT = D // P
SEQ, META = 512, 16
L = SEQ + META
HALF = L // 2
NFULL = SEQ // P
TAIL = L - NFULL * P
NTT = NFULL + 1
TOK = [P] * NFULL + [TAIL]
F = ((8 * D // 3 + 127) // 128) * 128
FT = F // P
DOWN_K = (8, 7, 7)
FOX_H, FOX_D = 16, 64
HG_H, HG_LEVELS = 8, 7
RET_H, RET_DK, RET_DV = 4, 256, 512
SB_SCALE = 64 ** -0.5
EPS, GN_EPS = 1e-6, 1e-5
RAW_SLOTS = 4

ROW_FOX, ROW_HGRN, ROW_FFN, ROW_LB = 0, 8, 16, 32
ROW_MIXPRE, ROW_MIXPOST, ROW_FFNPRE, ROW_FFNPOST = 48, 56, 64, 72
ROW_OGAIN, ROW_QGAIN, ROW_KGAIN, N_ROWS = 80, 81, 82, 83

STRIP_A, STRIP_B, STRIP_C = 0, 512, 1024
STRIP0 = (STRIP_A, STRIP_B, STRIP_C, STRIP_B + 3 * P)
TAILS = STRIP_C + 2 * P
N_STRIP = TAILS + NTT * TAIL
BANKS = ((0, 512), (512, 1024), (1024, N_STRIP))

ROWS0 = (0, 128, 384, 768, 1280)
N_ROWS0 = 1280 + L
SCORES0 = (0, 128, 512, 1536, 896)
TURNS = ((0, 1), (3,), (2, 4))
ORDER = [n for turn in TURNS for n in turn]


def tail_at(j):
    return TAILS + TAIL * j


class Phase:

    def __init__(self, before, n, groups):
        self.n, self.groups = n, groups
        self.upi, self.gpi = sum(map(len, groups)), len(groups)
        self.u0 = before.u0 + before.n * before.upi if before else 0
        self.g0 = before.g0 + before.n * before.gpi if before else 0
        assert n == 1 or (self.upi % RAW_SLOTS == 0 and self.gpi % 2 == 0)


K8, K4 = [[KT]] * 4, [[KT // 2]] * 8
PH_QK = Phase(None, 4, K8)
PH_V = Phase(PH_QK, 2, K8)
PH_FOXF = Phase(PH_V, 1, [[KT]])
PH_GATE = Phase(PH_FOXF, 2, K8)
PH_FOXOUT = Phase(PH_GATE, 2, K8)
PH_UP0 = Phase(PH_FOXOUT, FT // 2, K8)
PH_DOWN0 = Phase(PH_UP0, 2, [list(DOWN_K)] * 4)
PH_HGRN = Phase(PH_DOWN0, HG_H, K8)
PH_HGOUT = Phase(PH_HGRN, 2, K8)
PH_UP1 = Phase(PH_HGOUT, FT // 2, K8)
PH_DOWN1 = Phase(PH_UP1, 2, [list(DOWN_K)] * 4)
PH_RET = Phase(PH_DOWN1, RET_H, [[KT]] * 12 + K4)
PH_GA = Phase(PH_RET, 2, K8)
PH_SB = Phase(PH_GA, 6, K8)
PH_GB = Phase(PH_SB, 2, K8)
PH_SBOUT = Phase(PH_GB, 2, K8)
PH_OUT = Phase(PH_SBOUT, 2, K8)
PH_UP2 = Phase(PH_OUT, FT // 2, K8)
PH_DOWN2 = Phase(PH_UP2, 2, [list(DOWN_K)] * 4)


def tables():
    i = np.arange(P)
    bd = np.zeros((P, P), np.float32)
    bd[:64, :64] = bd[64:, 64:] = 1.0 / FOX_D
    square = np.stack([
        np.full((P, P), 1.0 / D), bd, np.full((P, P), 1.0 / P), np.full((P, P), 1.0 / RET_DV),
        np.eye(P), -(i[:, None] >= i[None, :]).astype(np.float32), -np.ones((P, P)),
        np.where(i[None, :] > i[:, None], 1e30, 0.0),
    ], 1).astype(np.float32)
    half = RET_DK // 2
    inv = np.float32(10000.0) ** (-np.arange(half, dtype=np.float32) / np.float32(half))
    ang = (inv[:, None] * np.arange(L, dtype=np.float32)[None, :]).astype(np.float32)
    rotary = np.stack([np.cos(ang), np.sin(ang)], 1).astype(np.float32)
    s, t = i[:, None], None
    dec = np.zeros((P, RET_H, N_STRIP), np.float64)
    for h in range(RET_H):
        lg = np.log1p(-(2.0 ** (-5.0 - h)))
        for j in range(NTT):
            key = P * j + s
            runs = [(tail_at(j), np.arange(NFULL * P, L))]
            if j < NFULL:
                runs.append((STRIP0[j], np.arange(P * j, NFULL * P)))
            for c, t in runs:
                gap = t[None, :] - key
                dec[:, h, c:c + len(t)] = np.where(gap >= 0, np.exp(lg * np.maximum(gap, 0)), 0.0) * RET_DK ** -0.5
    cols = np.arange(L) % P
    masks = np.zeros((P, HG_LEVELS + 1, L), np.float32)
    for n in range(HG_LEVELS):
        w = 1 << n
        masks[:, n] = (i[:, None] // (2 * w) == cols // (2 * w)) & (i[:, None] // w % 2 == 0) & (cols // w % 2 == 1)
    masks[:, HG_LEVELS] = i[:, None] == cols
    restart = np.broadcast_to((np.arange(L) % P != 0).astype(np.float32), (P, L)).copy()
    return {"t_square": square, "t_rotary": rotary, "t_decay": dec.astype(np.float32), "t_masks": masks,
            "t_restart": restart}


def build(nc, tens, out):
    ctx = ExitStack()
    with ctx:
        program(nc, ctx, tens, out)


def program(nc, ctx, dram, out):
    cursor = [16512]

    def place(name, shape, dtype=F32, at=None):
        size = int(np.prod(shape[1:])) * {F32: 4, F32R: 4, U8: 1}[dtype]
        size = (size + 31) // 32 * 32
        if at is None:
            at = cursor[0]
            cursor[0] += size
        return nc.alloc_sbuf_tensor_at(name, shape, dtype, offset=at), at + size

    def fixed(name, shape, dtype=F32):
        return place(name, shape, dtype)[0]

    class Area:

        def __init__(self, at, end):
            self.at, self.end = at, end

        def take(self, name, shape, dtype=F32):
            t, self.at = place(name, shape, dtype, self.at)
            assert self.at <= self.end, (name, self.at, self.end)
            return t

    h = fixed("h", [P, KT, L])
    x_at = cursor[0]
    xh = fixed("xh", [P, KT, L], F32R)
    xl = fixed("xl", [P, KT, L], F32R)
    x_end = cursor[0]
    raw = fixed("raw", [P, RAW_SLOTS, KT, P])
    wh = fixed("wh", [P, 2, KT, P], F32R)
    wl = fixed("wl", [P, 2, KT, P], F32R)
    square = fixed("square", [P, 8, P])
    mean_d, mean_64, mean_128, mean_512, ident, neg_tri, neg_one, future = (square[:, n, :] for n in range(8))
    gains = fixed("gains", [P, N_ROWS])
    conv = fixed("conv", [P, 2, 4 * FT])
    meta2 = fixed("meta2", [P, KT, META])
    small = fixed("small", [P, 104])
    eps, gn_eps, one = small[:, 0:1], small[:, 1:2], small[:, 2:3]
    floor, span, bf = small[:, 8:16], small[:, 16:24], small[0:FOX_H, 3:4]
    rowmin, rowsum, rowinv = small[:, 24:34], small[:, 34:44], small[:, 44:54]
    exp_tot = small[:, 54:58]
    lb = small[:, 64:104].rearrange("p (a n) -> p a n", a=5)
    norms_at = cursor[0]
    ssq = fixed("ssq", [P, L])
    rstd = fixed("rstd", [P, L])
    lnt = fixed("lnt", [P, L])
    sq = fixed("sq", [P, 2, L])
    post_t = fixed("post_t", [P, 2, L])
    arena, end = cursor[0], 229344

    a = Area(arena, end)
    x_tok = a.take("x_tok", [P, NFULL, D])
    m_tok = a.take("m_tok", [META, 2, D])
    rows = a.take("rows", [P, P])
    crows = a.take("crows", [P, 2, P])

    a = Area(arena, end)
    heads = a.take("heads", [P, 32, L])
    fx = place("fx", [FOX_H, 4, L], F32, a.at)[0]
    masks_f = place("masks_f", [P, HG_LEVELS + 1, L], F32, a.at)[0]
    yh = a.take("yh", [P, KT, L], F32R)
    yl = a.take("yl", [P, KT, L], F32R)
    rest = a.at
    a = Area(rest, end)
    crep = a.take("crep", [P, 2, L])
    o_t = a.take("o_t", [P, L])
    a = Area(x_at, x_end)
    t_rows = a.take("t_rows", [P, 2, N_ROWS0])
    p_t = a.take("p_t", [P, N_STRIP])
    v_t = a.take("v_t", [P, NTT, P])
    q_s = a.take("q_s", [P, L])
    k_s = a.take("k_s", [P, L])
    v_s = a.take("v_s", [P, L])

    a = Area(rest, end)
    masks = a.take("masks", [P, HG_LEVELS + 1, L], U8)
    restart = a.take("restart", [P, L])
    g_f, g_lf, g_b = lnt, post_t[:, 0, :], post_t[:, 1, :]
    a = Area(x_at, x_end)
    g_q = a.take("g_q", [P, L])
    g_k = a.take("g_k", [P, NTT * P])
    g_v, g_o, g_r = sq[:, 1, :], rstd, ssq
    g_d = a.take("g_d", [P, 2, L])
    g_e = a.take("g_e", [P, 2, L])
    g_qk = a.take("g_qk", [P, 2, NTT * P])
    g_diag = a.take("g_diag", [P, L])
    g_off = a.take("g_off", [P, N_STRIP])
    g_vt = a.take("g_vt", [P, NTT, P])
    g_left = a.take("g_left", [P, 10, P])

    def ffn_area(n, at):
        a = Area(at, end)
        hidden = a.take(f"hidh{n}", [P, FT, L], F32R), a.take(f"hidl{n}", [P, FT, L], F32R)
        pre = a.take(f"pre{n}", [P, 2, L + 2])
        t1 = a.take(f"t1{n}", [P, 2, L])
        t2 = a.take(f"t2{n}", [P, L])
        b = Area(x_at, x_end)
        return hidden, pre, t1, t2, b.take(f"ff{n}", [P, KT, L]) if n == 2 else None

    ffn = [ffn_area(n, arena) for n in range(3)]

    a = Area(arena, end)
    yr = a.take("yr", [P, KT, L])
    after_yr = a.at
    rt = a.take("rt", [P, 12, L])
    rh = a.take("rh", [P, KT // 2, L], F32R)
    rl = a.take("rl", [P, KT // 2, L], F32R)
    r_vt = a.take("r_vt", [P, NTT, RET_DV])
    r_s = a.take("r_s", [P, N_STRIP])
    decay = a.take("decay", [P, N_STRIP])
    rotary = a.take("rotary", [P, 2, L])
    r_t = a.take("r_t", [P, 2, L])
    r_y = a.take("r_y", [P, 4, L])
    r_sum = a.take("r_sum", [P, L])

    a = Area(after_yr, end)
    sb = a.take("sb", [P, 24, L])
    gb = a.take("gb", [P, KT, L])
    s_v = a.take("s_v", [P, L])
    s_k = a.take("s_k", [P, NTT * P])
    s_vt = a.take("s_vt", [P, NTT, P])
    s_e = a.take("s_e", [P, N_STRIP])
    s_sp = a.take("s_sp", [P, 2, N_STRIP])
    a = Area(norms_at, arena)
    s_a = a.take("s_a", [P, 2, N_STRIP])
    s_q = a.take("s_q", [P, L])
    a = Area(after_yr, end)
    mh = a.take("mh", [P, KT, L], F32R)
    ml = a.take("ml", [P, KT, L], F32R)
    m_t = a.take("m_t", [P, 2, L])
    mix = yr
    a = Area(arena, end)
    o_tok = a.take("o_tok", [P, 2, D])

    ps = ctx.enter_context(nc.psum_tensor("ps", [P, 8, 512], F32))
    flat = ps[:, :, :].rearrange("p b n -> p (b n)")
    scratch = nc.dram_tensor("c_scratch", (FOX_H, L), F32, kind="Internal").ap()

    sems = {}

    def s(name):
        if name not in sems:
            sems[name] = ctx.enter_context(nc.semaphore(name))
        return sems[name]

    def row(t, n):
        return t[:, n, :] if isinstance(n, int) else t[:, bass.ds(n, 1), :].rearrange("p a t -> p (a t)")

    def halves(t, n):
        if isinstance(n, int):
            return t[:, n, :].rearrange("p (g t) -> p g t", g=2)
        return t[:, bass.ds(n, 1), :].rearrange("p a (g t) -> p (a g) t", g=2)

    def col(t, n):
        return t[:, n:n + 1] if isinstance(n, int) else t[:, bass.ds(n, 1)]

    def two(t):
        return t.rearrange("p (g t) -> p g t", g=2)

    def pair(b):
        return ps[:, b:b + 2, 0:HALF]

    def out_pair(g):
        return pair(2 * (g % 2))

    def carry(eng, name):
        eng.sem_inc(s(name), 1)

    def loop(eng, n, body, start=0):
        if n - start == 1:
            body(start)
        else:
            with eng.Fori(start, n) as i:
                body(i)

    def tables_for(act, name):
        act.preload_act_table_set({"ln_exp": "natural_log_exp_and_others", "sigmoid": "sigmoid_and_others",
                                   "silu": "silu_and_others"}[name])

    def unit(ph, i, uj):
        return ph.u0 + uj + ph.upi * i

    def unit_sizes(ph):
        return [k for g in ph.groups for k in g]

    def sp_unit(sp, ph, i, uj, src):
        u = unit(ph, i, uj)
        nk = unit_sizes(ph)[uj]
        sp.wait_ge(s("w_split"), u + 1)
        sp.dma_start(raw[:, (ph.u0 + uj) % RAW_SLOTS, 0:nk, :], src)\
            .then_inc(s(f"w_loaded{(ph.u0 + uj) % RAW_SLOTS}"), 16)

    def ahead(ph, i, uj, last):
        sizes = unit_sizes(ph)
        if last and uj + 1 == len(sizes):
            return None
        v = ph.u0 + uj + 1
        nk = sizes[uj + 1] if uj + 1 < len(sizes) else KT
        return v, v + ph.upi * i, v // RAW_SLOTS + 1 + (ph.upi // RAW_SLOTS) * i, nk

    def act_hi(act, v, u, count, nk):
        act.wait_ge(s(f"w_loaded{v % RAW_SLOTS}"), 16 * count)
        act.wait_ge(s("mm_done"), u + 1)
        nc.scalar.activation(wh[:, v % 2, 0:nk, :], raw[:, v % RAW_SLOTS, 0:nk, :], ACT.Copy).then_inc(s("w_hi"), 1)

    def dve_lo(dve, v, u, count, nk):
        dve.wait_ge(s("w_hi"), u + 1)
        nc.vector.tensor_tensor(wl[:, v % 2, 0:nk, :], raw[:, v % RAW_SLOTS, 0:nk, :],
                                wh[:, v % 2, 0:nk, :].bitcast(F32), ALU.subtract).then_inc(s("w_split"), 1)

    def split_ahead(eng, f, ph, i, uj, last=False):
        nxt = ahead(ph, i, uj, last)
        if nxt:
            f(eng, *nxt)

    def group_end(ph, i, gj):
        return 2 + unit(ph, i, sum(map(len, ph.groups[:gj + 1])))

    def pe_group(pe, ph, i, gj, hi, lo, ready=None):
        bank = 2 * ((ph.g0 + gj) % 2)
        pe.wait_ge(s("psum_free"), ph.g0 + gj + 1 + ph.gpi * i)
        uj = sum(map(len, ph.groups[:gj]))
        k, n_k = 0, sum(ph.groups[gj])
        for nk in ph.groups[gj]:
            slot = (ph.u0 + uj) % 2
            pe.wait_ge(s("w_split"), unit(ph, i, uj) + RAW_SLOTS + 1)
            for kk in range(nk):
                if ready:
                    pe.wait_ge(s(ready[0]), ready[1] + k + 1)
                for n, (w, x) in enumerate(((wh, hi), (wh, lo), (wl, hi))):
                    for b in range(2):
                        last = nc.tensor.matmul(ps[:, bank + b, 0:HALF], w[:, slot, kk, :],
                                                x[:, k, b * HALF:(b + 1) * HALF],
                                                start=(k == 0 and n == 0), stop=(k == n_k - 1 and n == 2))
                k += 1
            last.then_inc(s("mm_done"), 1)
            uj += 1

    def evacuated(ph, i, gj):
        return ph.g0 + gj + 3 + ph.gpi * i

    def act_x(act, r, m, mm, gain_row, done):
        act.wait_ge(s(done[0]), done[1])
        if not isinstance(m, int):
            carry(act, "act_carry")
        nc.scalar.activation(row(xh, m), row(h, m), ACT.Copy, scale=col(gains, m + gain_row)).then_inc(s("xh_ready"), 1)
        act_square(act, r, m, mm, row(h, m))

    def act_square(act, r, m, mm, src):
        act.wait_ge(s("sq_used"), KT * r + 1 + m)
        if not isinstance(m, int):
            carry(act, "act_carry")
        nc.scalar.activation(sq[:, mm % 2, :], src, ACT.Square).then_inc(s("sq_ready"), 1)

    def dve_x(dve, rx, m, gain_row):
        dve.wait_ge(s("xh_ready"), KT * rx + 1 + m)
        nc.vector.scalar_tensor_tensor(row(xl, m), row(h, m), col(gains, m + gain_row), row(xh, m).bitcast(F32),
                                       ALU.mult, ALU.subtract).then_inc(s("x_ready"), 1)

    def pool_ssq(pool, r):
        if r:
            pool.wait_ge(s("ssum"), r)
        for m in range(KT):
            pool.wait_ge(s("sq_ready"), KT * r + m + 1)
            if m:
                pool.wait_ge(s("sq_used"), KT * r + m + 2)
                nc.gpsimd.tensor_tensor(ssq[:, :], ssq[:, :], sq[:, m % 2, :], ALU.add).then_inc(s("sq_used"), 1)
            else:
                nc.gpsimd.tensor_copy(ssq[:, :], sq[:, 0, :]).then_inc(s("sq_used"), 1)

    def pe_sum(pe, r):
        pe.wait_ge(s("sq_used"), KT * (r + 1) + 2)
        for b in range(2):
            last = nc.tensor.matmul(ps[:, 4 + b, 0:HALF], mean_d, ssq[:, b * HALF:(b + 1) * HALF], start=True, stop=True)
        last.then_inc(s("ssum"), 1)

    def act_rsqrt(act, src, dst, tmp, bias, chain, n):
        nc.scalar.activation(tmp, src, ACT.Ln, bias=bias).then_inc(s(chain), 1)
        act.wait_ge(s(chain), n + 1)
        return nc.scalar.activation(dst, tmp, ACT.Exp, scale=-0.5)

    def act_rstd(act, r):
        tables_for(act, "ln_exp")
        act.wait_ge(s("ssum"), r + 1)
        act_rsqrt(act, pair(4), two(rstd[:, :]), two(lnt[:, :]), eps, "rstd_ln", r).then_inc(s("rstd_ready"), 1)

    def dve_add_h(dve, ph, i, mm, skip=0):
        dve.wait_ge(s("mm_done"), group_end(ph, i, mm))
        m = 4 * i + mm
        pv = out_pair(ph.g0 + mm)
        if skip:
            hm = row(h, m)
            nc.vector.tensor_tensor(hm[:, HALF:L], hm[:, HALF:L], pv[:, 1, :], ALU.add).then_inc(s("h_half"), 1)
            dve.wait_ge(s("h_half"), 4 * i + mm + 1)
            nc.vector.tensor_tensor(hm[:, skip:HALF], hm[:, skip:HALF], pv[:, 0, skip:HALF], ALU.add)\
                .then_inc(s("psum_free"), 1)
        else:
            nc.vector.tensor_tensor(halves(h, m), halves(h, m), pv, ALU.add).then_inc(s("psum_free"), 1)

    def post_norm(dve, src, post_row, r, n0, name, rx, next_row):
        dve.wait_ge(s("rstd_ready"), r + 1)
        for m in range(KT + 1):
            if m < KT:
                nc.vector.scalar_tensor_tensor(post_t[:, m % 2, :], row(src, m), col(gains, post_row + m), rstd[:, :],
                                               ALU.mult, ALU.mult).then_inc(s("post_scaled"), 1)
                dve.wait_ge(s("post_scaled"), n0 + m + 1)
                nc.vector.tensor_tensor(row(h, m), row(h, m), post_t[:, m % 2, :], ALU.add).then_inc(s(name), 1)
            if m and rx is not None:
                dve_x(dve, rx, m - 1, next_row)

    def hgrn_level(n):
        w = HG_LEVELS - 1 - n
        return 1 << w, L if w <= 3 else SEQ

    def hgrn_distance(eng, n):
        width, cols_ = hgrn_level(n)
        b = g_b[:, 0:cols_].rearrange("p (b t) -> p b t", t=2 * width)
        return eng.tensor_tensor(g_d[:, n % 2, 0:cols_].rearrange("p (b t) -> p b t", t=2 * width), b,
                                 b[:, :, width - 1:width].to_broadcast([P, cols_ // (2 * width), 2 * width]),
                                 ALU.subtract)

    block = ctx.enter_context(nc.Block())

    @block.sync
    def _(sp):
        rows8 = (("fox_norm", ROW_FOX, 8), ("hgrn_norm", ROW_HGRN, 8), ("ffn_norm", ROW_FFN, 16),
                 ("hgrn_lower_bounds", ROW_LB, 16), ("norm_mix_pre_2", ROW_MIXPRE, 8),
                 ("norm_mix_post_2", ROW_MIXPOST, 8), ("norm_ffn_pre_2", ROW_FFNPRE, 8),
                 ("norm_ffn_post_2", ROW_FFNPOST, 8), ("hgrn_o_gain", ROW_OGAIN, 1))
        for name, r, n in rows8:
            sp.dma_start(rows[r:r + n, :], dram[name].rearrange("a (b n) -> (a b) n", n=P)).then_inc(s("rows_loaded"), 16)
        for name, r in (("fox_q_gain", ROW_QGAIN), ("fox_k_gain", ROW_KGAIN)):
            for half in range(2):
                sp.dma_start(rows[r:r + 1, 64 * half:64 * half + 64], dram[name]).then_inc(s("rows_loaded"), 16)
        for l in range(2):
            sp.dma_start(crows[0:3 * FT, l, :], dram["ffn_conv_w"][l].rearrange("c (b n) -> (c b) n", n=P))\
                .then_inc(s("rows_loaded"), 16)
            sp.dma_start(crows[3 * FT:4 * FT, l, :], dram["ffn_conv_b"][l:l + 1, :].rearrange("c (b n) -> (c b) n", n=P))\
                .then_inc(s("rows_loaded"), 16)
        sp.dma_start(bf, dram["fox_b_f"].rearrange("a n -> n a")).then_inc(s("rows_loaded"), 16)

        def stream(ph, src):
            def body(i):
                for uj in range(ph.upi):
                    sp_unit(sp, ph, i, uj, src(i, uj))
            loop(sp, ph.n, body)

        def cols(w, first, step, k0=0, nk=KT):
            rows_ = w[P * k0:P * (k0 + nk), :].rearrange("(k p) n -> p k n", p=P)
            return lambda i, c: rows_[:, :, bass.ds(i * step + (first + c), P)] if not isinstance(i, int) \
                else rows_[:, :, first + c + i * step:first + c + i * step + P]

        def dense(ph, w, first):
            f = cols(w, first, 4 * P)
            stream(ph, lambda i, uj: f(i, P * uj))

        def up(ph, gate, up_):
            fg, fu = cols(gate, 0, 2 * P), cols(up_, 0, 2 * P)
            stream(ph, lambda i, uj: (fu if uj % 2 else fg)(i, P * (uj // 2)))

        def down(ph, w):
            k0 = [sum(DOWN_K[:n]) for n in range(3)]
            f = [cols(w, 0, 4 * P, k0[n], DOWN_K[n]) for n in range(3)]
            stream(ph, lambda i, uj: f[uj % 3](i, P * (uj // 3)))

        fox = dram["fox_w_in"][0]
        dense(PH_QK, fox, 0)
        dense(PH_V, fox, 2 * D)
        dense(PH_FOXF, fox, 3 * D)
        dense(PH_GATE, fox, 3 * D + FOX_H)
        dense(PH_FOXOUT, dram["fox_w_out"][0], 0)
        up(PH_UP0, dram["ffn_w_gate"][0], dram["ffn_w_up"][0])
        down(PH_DOWN0, dram["ffn_w_down"][0])
        f = cols(dram["hgrn_w_in"][0], 0, P)
        stream(PH_HGRN, lambda i, uj: f(i, D * uj))
        dense(PH_HGOUT, dram["hgrn_w_out"][0], 0)
        up(PH_UP1, dram["ffn_w_gate"][1], dram["ffn_w_up"][1])
        down(PH_DOWN1, dram["ffn_w_down"][1])
        w_in = dram["w_in_2"][0]
        q_at, k_at, v_at, g_at = 0, D, 2 * D, 4 * D
        parts = [(q_at, 2 * P, 2), (k_at, 2 * P, 2), (v_at, 4 * P, 4), (g_at, 4 * P, 4)]
        units = [cols(w_in, first + P * n, step) for first, step, count in parts for n in range(count)]
        out_rows = dram["w_ret_out_2"][0].rearrange("(r k p) n -> r p k n", p=P, k=KT // 2)

        def ret(i):
            for uj in range(12):
                sp_unit(sp, PH_RET, i, uj, units[uj](i, 0))
            for m in range(KT):
                sp_unit(sp, PH_RET, i, 12 + m,
                        out_rows[bass.ds(i, 1), :, :, m * P:(m + 1) * P].rearrange("r p k n -> p (r k) n"))
        loop(sp, RET_H, ret)
        dense(PH_GA, w_in, 9 * D)
        dense(PH_SB, w_in, 6 * D)
        dense(PH_GB, w_in, 10 * D)
        dense(PH_SBOUT, dram["w_sb_out_2"][0], 0)
        dense(PH_OUT, dram["w_out_2"][0], 0)
        up(PH_UP2, dram["w_ffn_in_2"][0][:, 0:F], dram["w_ffn_in_2"][0][:, F:2 * F])
        down(PH_DOWN2, dram["w_ffn_out_2"][0])
        for c in range(NFULL):
            sp.wait_ge(s("o_tok_ready"), 2 * (c + 1))
            sp.dma_start(out[0, P * c:P * (c + 1), :], o_tok[:, c % 2, :]).then_inc(s(f"stored{c % 2}"), 16)
        for c in range(2):
            sp.wait_ge(s(f"stored{c}"), 16 * NFULL // 2)

    def causal_pv(out_main, out_tail, vt, pt, width):
        for j in range(NFULL):
            nc.tensor.matmul(out_main(P * j), vt(j, P), pt[:, STRIP0[j]:STRIP0[j] + SEQ - P * j],
                             start=(j == 0), stop=(j == NFULL - 1))
        for j in range(NTT):
            k = TOK[j]
            last = nc.tensor.matmul(out_tail, vt(j, k), pt[0:k, tail_at(j):tail_at(j) + TAIL],
                                    start=(j == 0), stop=(j == NFULL))
        return last

    def transposes(src, bank, rows_=P):
        for j in range(NTT):
            w = TOK[j]
            last = nc.tensor.transpose(ps[0:w, bank + j // NFULL, P * (j % NFULL):P * (j % NFULL) + P],
                                       src[:, P * j:P * j + w], ident)
        return last

    @block.tensor
    def _(pe):
        pe.wait_ge(s("square_loaded"), 16)
        pe.wait_ge(s("m_loaded"), 32)
        for n in range(2):
            for m in range(KT):
                last = nc.tensor.transpose(ps[:, 3, P * n + META * m:P * n + META * (m + 1)],
                                           m_tok[:, n, P * m:P * (m + 1)], ident[0:META, 0:META])
        last.then_inc(s("x_t"), 1)
        for c in range(NFULL):
            pe.wait_ge(s(f"x_loaded{c}"), 16)
            for g in range(2):
                b = 2 * c + g
                if b >= 4:
                    pe.wait_ge(s("h_init"), b - 2)
                for m in range(4):
                    last = nc.tensor.transpose(ps[:, 4 + b % 4, P * m:P * (m + 1)],
                                               x_tok[:, c, P * (4 * g + m):P * (4 * g + m + 1)], ident)
                last.then_inc(s("x_t"), 1)
        pe.wait_ge(s("rows_loaded"), 16 * 18)
        nc.tensor.transpose(ps[:, 0, 0:N_ROWS], rows[0:N_ROWS, :], ident[0:N_ROWS, 0:N_ROWS])
        for l in range(2):
            last = nc.tensor.transpose(ps[:, 1 + l, 0:4 * FT], crows[0:4 * FT, l, :], ident[0:4 * FT, 0:4 * FT])
        last.then_inc(s("rows_t"), 1)
        pe.wait_ge(s("rows_taken"), 1)
        pe.wait_ge(s("h_init"), 9)

        def dense(ph, hi, lo, ready, sums=None):
            def body(i):
                for gj in range(ph.gpi):
                    pe_group(pe, ph, i, gj, hi, lo, ready if gj == 0 else None)
                    if sums is not None and isinstance(i, int) and i + gj == 0:
                        pe_sum(pe, sums)
            if sums is not None:
                body(0)
            loop(pe, ph.n, body, 0 if sums is None else 1)

        def feed_forward(n, up, down, rx, sums):
            hidden = ffn[n][0]
            dense(up, xh, xl, ("x_ready", KT * rx), sums)
            dense(down, *hidden, ("hid_ready", FT * n))

        dense(PH_QK, xh, xl, ("x_ready", 0), 0)

        def values(i):
            for gj in range(4):
                m = 4 * i + gj
                for j in range(2):
                    pe.wait_ge(s("qn_sq"), 2 * m + j + 1)
                    for b in range(2):
                        last = nc.tensor.matmul(ps[:, 4 + 2 * j + b, 0:HALF], mean_64, sq[:, j, b * HALF:(b + 1) * HALF],
                                                start=True, stop=True)
                    last.then_inc(s("qn_sum"), 1)
                pe_group(pe, PH_V, i, gj, xh, xl)
        loop(pe, PH_V.n, values)
        dense(PH_FOXF, xh, xl, None)
        dense(PH_GATE, xh, xl, None)
        pe.wait_ge(s("psum_free"), PH_FOXOUT.g0 + 2)

        def scores(i, b):
            lo, hi = FOX_D * b, FOX_D * (b + 1)
            before = 0
            for turn in TURNS:
                before += len(turn)
                if b:
                    pe.wait_ge(s("t_min"), 10 * i + before)
                for n in turn:
                    w = TOK[n]
                    runs = ((0, P * n + w),) if n < NFULL else ((0, P), (P, L))
                    for k0, k1 in runs:
                        nc.tensor.matmul(flat[0:w, SCORES0[n] + k0:SCORES0[n] + k1], q_s[lo:hi, P * n:P * n + w],
                                         k_s[lo:hi, k0:k1], start=True, stop=(k1 <= P * n))
                    last = nc.tensor.matmul(flat[0:w, SCORES0[n] + P * n:SCORES0[n] + P * n + w], ident[:, 0:w],
                                            future[:, 0:w], start=False, stop=True)
                last.then_inc(s("s_done"), 1)

        def pair_(i):
            pe.wait_ge(s("qk_staged"), 2 * i + 2)
            scores(i, 0)
            scores(i, 1)
            pe.wait_ge(s("v_staged"), i + 1)
            transposes(v_s, 4).then_inc(s("vt_mm"), 1)
            for b in range(2):
                if b == 0:
                    pe.wait_ge(s("vt_ready"), i + 1)
                    pe.wait_ge(s("o_done"), i + 1)
                pe.wait_ge(s("p_norm"), 2 * i + b + 3)
                for n in range(NTT):
                    w = TOK[n]
                    for j in range(n + 1):
                        at = STRIP0[j] + P * (n - j) if n < NFULL else tail_at(j)
                        last = nc.tensor.transpose(flat[0:TOK[j], 2048 + at:2048 + at + w],
                                                   t_rows[0:w, b, ROWS0[n] + P * j:ROWS0[n] + P * j + TOK[j]],
                                                   ident[0:w, 0:w])
                last.then_inc(s("pt_mm"), 1)
                pe.wait_ge(s("pt_a"), 2 * i + b + 1)
                pe.wait_ge(s("pt_b"), 2 * i + b + 1)
                lo, hi = FOX_D * b, FOX_D * (b + 1)
                causal_pv(lambda t: ps[lo:hi, 7, t:SEQ], ps[lo:hi, 6, 496:512],
                          lambda j, k: v_t[0:k, j, lo:hi], p_t, FOX_D).then_inc(s("o_mm"), 1)
        loop(pe, FOX_H // 2, pair_)
        dense(PH_FOXOUT, yh, yl, ("y_ready", 0))
        feed_forward(0, PH_UP0, PH_DOWN0, 1, 1)

        dense(PH_HGRN, xh, xl, ("x_ready", KT * 2), 2)
        pe.wait_ge(s("psum_free"), PH_HGOUT.g0 + 2)

        def hgrn_sum(i):
            pe.wait_ge(s("g_o_sq"), i + 1)
            for b in range(2):
                last = nc.tensor.matmul(ps[:, 4 + b, 0:HALF], mean_128, sq[:, 0, b * HALF:(b + 1) * HALF], start=True, stop=True)
            last.then_inc(s("g_o_sum"), 1)

        def hgrn(i):
            pe.wait_ge(s("g_staged"), i + 1)
            transposes(g_v, 4).then_inc(s("g_vt_mm"), 1)
            for n in range(HG_LEVELS + 1):
                w = HG_LEVELS - 1 - n
                pr = 2 * (n % 2)
                if n >= 2:
                    pe.wait_ge(s("g_lv_used"), (HG_LEVELS + 1) * i + n - 1)
                if n < HG_LEVELS:
                    pe.wait_ge(s("g_qk_ready"), HG_LEVELS * i + n + 1)
                    left = right = g_qk[:, n % 2, :]
                else:
                    left, right = g_k, g_q
                for c in range(NTT if w <= 3 else NFULL):
                    k = TOK[c]
                    last = nc.tensor.matmul(ps[:, pr + c // NFULL, P * (c % NFULL):P * (c % NFULL) + k],
                                            left[:, P * c:P * c + P], right[:, P * c:P * c + k], start=True, stop=True)
                last.then_inc(s("g_lv_mm"), 1)
                if n == 3 and not isinstance(i, int):
                    pe.wait_ge(s("g_vt_ready"), i + 1)
                    hgrn_sum(i - 1)
            pe.wait_ge(s("g_vt_ready"), i + 1)
            pe.wait_ge(s("g_left_ready"), i + 1)
            if not isinstance(i, int):
                pe.wait_ge(s("g_r_ready"), i)
            for j in range(1, NTT):
                for c in range(j):
                    at = STRIP0[c] + P * (j - c) if j < NFULL else tail_at(c)
                    last = nc.tensor.matmul(flat[:, 2048 + at:2048 + at + TOK[j]], g_left[:, j * (j - 1) // 2 + c, :],
                                            g_f[:, P * j:P * j + TOK[j]], start=True, stop=True)
            last.then_inc(s("g_off_mm"), 1)
            pe.wait_ge(s("g_off_ready"), i + 1)
            if not isinstance(i, int):
                pe.wait_ge(s("g_o_ready"), i)
            pe.wait_ge(s("g_lv_used"), (HG_LEVELS + 1) * (i + 1))
            for c in range(NFULL):
                nc.tensor.matmul(ps[:, 7, P * c:P * (c + 1)], g_vt[:, c, :], g_diag[:, P * c:P * (c + 1)],
                                 start=(c == 0), stop=False, skip_group_check=True)
            for c in range(NFULL - 1):
                nc.tensor.matmul(ps[:, 7, P * (c + 1):SEQ], g_vt[:, c, :],
                                 g_off[:, STRIP0[c] + P:STRIP0[c] + SEQ - P * c],
                                 start=False, stop=(c == NFULL - 2), skip_group_check=True)
            for c in range(NFULL):
                nc.tensor.matmul(ps[:, 6, 496:512], g_vt[:, c, :], g_off[:, tail_at(c):tail_at(c) + TAIL],
                                 start=(c == 0), stop=False)
            nc.tensor.matmul(ps[:, 6, 496:512], g_vt[0:TAIL, NFULL, :], g_diag[0:TAIL, SEQ:L],
                             start=False, stop=True).then_inc(s("g_o_mm"), 1)
        hgrn(0)
        loop(pe, HG_H, hgrn, 1)
        hgrn_sum(HG_H - 1)
        dense(PH_HGOUT, yh, yl, ("y_ready", KT))
        feed_forward(1, PH_UP1, PH_DOWN1, 3, 3)

        def ret(i):
            for gj in range(8):
                pe_group(pe, PH_RET, i, gj, xh, xl, ("x_ready", KT * 4) if gj == 0 else None)
                if isinstance(i, int) and i + gj == 0:
                    pe_sum(pe, 4)
            pe.wait_ge(s("psum_free"), evacuated(PH_RET, i, 7))
            for e in range(4):
                for j in range(NFULL):
                    last = nc.tensor.transpose(ps[:, 4 + j, P * e:P * (e + 1)], rt[:, 4 + e, P * j:P * j + P], ident)
            last.then_inc(s("r_vt_mm"), 1)
            pe.wait_ge(s("r_vt_ready"), 2 * i + 1)
            for e in range(4):
                last = nc.tensor.transpose(ps[0:TAIL, 7, P * e:P * (e + 1)], rt[:, 4 + e, SEQ:L], ident)
            last.then_inc(s("r_vt_mm"), 1)
            pe.wait_ge(s("r_rot"), i + 1)
            for c in range(2):
                for j in (0, 1, 3, 2):
                    first = c == 0 and j != 3
                    nc.tensor.matmul(flat[:, 2048 + STRIP0[j]:2048 + STRIP0[j] + SEQ - P * j],
                                     rt[:, 2 + c, P * j:P * j + P], rt[:, c, P * j:SEQ],
                                     start=first, stop=(c == 1), skip_group_check=True)
                for j in range(NTT):
                    last = nc.tensor.matmul(flat[0:TOK[j], 2048 + tail_at(j):2048 + tail_at(j) + TAIL],
                                            rt[:, 2 + c, P * j:P * j + TOK[j]], rt[:, c, SEQ:L],
                                            start=False, stop=(c == 1), skip_group_check=True)
            last.then_inc(s("r_s_mm"), 1)
            pe.wait_ge(s("r_s_ready"), i + 2)
            pe.wait_ge(s("r_vt_ready"), 2 * i + 2)
            for e in range(4):
                for j in range(NFULL):
                    last = nc.tensor.matmul(ps[:, 4 + e, P * j:SEQ], r_vt[:, j, P * e:P * (e + 1)],
                                            r_s[:, STRIP0[j]:STRIP0[j] + SEQ - P * j], start=(j == 0), stop=(j == NFULL - 1))
            last.then_inc(s("r_y_mm"), 1)
            pe.wait_ge(s("r_y_ready"), 2 * i + 1)
            for e in range(4):
                for j in range(NTT):
                    k = TOK[j]
                    last = nc.tensor.matmul(ps[:, 4, TAIL * e:TAIL * (e + 1)], r_vt[0:k, j, P * e:P * (e + 1)],
                                            r_s[0:k, tail_at(j):tail_at(j) + TAIL], start=(j == 0), stop=(j == NFULL))
            last.then_inc(s("r_y_mm"), 1)

            def mean(n, name):
                pe.wait_ge(s("r_sum_ready"), 2 * i + n + 1)
                for b in range(2):
                    last = nc.tensor.matmul(ps[:, 5 + b, 0:HALF], mean_512, r_sum[:, b * HALF:(b + 1) * HALF],
                                            start=True, stop=True)
                last.then_inc(s(name), 1)
            pe_group(pe, PH_RET, i, 8, xh, xl)
            mean(0, "r_mu_mm")
            pe_group(pe, PH_RET, i, 9, xh, xl)
            pe_group(pe, PH_RET, i, 10, xh, xl)
            mean(1, "r_var_mm")
            pe_group(pe, PH_RET, i, 11, xh, xl)
            pe.wait_ge(s("r_out_ready"), 4 * i + 4)
            for m in range(KT):
                pe_group(pe, PH_RET, i, 12 + m, rh, rl)
        ret(0)
        loop(pe, RET_H, ret, 1)
        dense(PH_GA, xh, xl, None)

        dense(PH_SB, xh, xl, None)
        dense(PH_GB, xh, xl, None)
        pe.wait_ge(s("psum_free"), PH_SBOUT.g0 + 2)

        def sb_z(b):
            lo, hi, z = FOX_D * b, FOX_D * (b + 1), 1536 * b
            for j in (0, 1, 3, 2):
                nc.tensor.matmul(flat[:, z + STRIP0[j]:z + STRIP0[j] + SEQ - P * j], s_k[lo:hi, P * j:P * j + P],
                                 s_q[lo:hi, P * j:SEQ], start=(j != 3), stop=False, skip_group_check=True)
            for j in range(NTT):
                last = nc.tensor.matmul(flat[:, z + tail_at(j):z + tail_at(j) + TAIL], s_k[lo:hi, P * j:P * j + P],
                                        s_q[lo:hi, SEQ:L], start=False, stop=False, skip_group_check=True)
            last.then_inc(s("sb_z"), 1)

        def sb_pair(i):
            pe.wait_ge(s("sb_v"), i + 1)
            pe.wait_ge(s("sb_o_done"), i + 1)
            transposes(s_v, 6).then_inc(s("sb_vt_mm"), 1)
            for b in range(2):
                z = 1536 * b
                pe.wait_ge(s("sb_spm"), 2 * i + b + 1)

                def minus(w, dst, src, last=False):
                    return nc.tensor.matmul(dst, w, src, start=False, stop=last, skip_group_check=True)
                for c0, c1 in BANKS:
                    minus(neg_tri, flat[:, z + c0:z + c1], s_sp[:, b, c0:c1])
                for n in range(1, NFULL):
                    src = s_sp[:, b, STRIP0[n]:STRIP0[n] + SEQ - P * n]
                    for j in range(n):
                        at = z + STRIP0[j] + P * (n - j)
                        minus(neg_one, flat[:, at:at + SEQ - P * n], src)
                for n in range(1, NTT):
                    for j in range(n):
                        last = minus(neg_one, flat[:, z + tail_at(j):z + tail_at(j) + TAIL],
                                     s_sp[:, b, tail_at(n):tail_at(n) + TAIL], True)
                last.then_inc(s("sb_acc"), 1)
            pe.wait_ge(s("sb_staged"), 2 * i + 4)
            for b in range(2):
                lo, hi = FOX_D * b, FOX_D * (b + 1)
                pe.wait_ge(s("sb_a"), 2 * i + b + 1)
                sb_z(b)
                pe.wait_ge(s("sb_am"), 2 * i + b + 1)
                if b == 0:
                    pe.wait_ge(s("sb_vt_ready"), i + 1)
                causal_pv(lambda t: ps[lo:hi, 6, t:SEQ], ps[lo:hi, 7, P:P + TAIL],
                          lambda j, k: s_vt[0:k, j, lo:hi], s_a[:, b, :], FOX_D).then_inc(s("sb_o_mm"), 1)
        pe.wait_ge(s("sb_staged"), 2)
        sb_z(0)
        sb_z(1)
        loop(pe, FOX_H // 2, sb_pair)
        dense(PH_SBOUT, xh, xl, ("sb_o_done", 1))
        dense(PH_OUT, mh, ml, ("m_ready", 0))
        pe_sum(pe, 5)
        feed_forward(2, PH_UP2, PH_DOWN2, 5, 6)
        pe_sum(pe, 7)
        for c in range(NFULL):
            for g in range(2):
                b = 2 * c + g
                pe.wait_ge(s("out_ready"), KT)
                if b >= 4:
                    pe.wait_ge(s("o_tok_ready"), b - 3)
                for m in range(4):
                    last = nc.tensor.transpose(ps[:, 4 + b % 4, P * m:P * (m + 1)],
                                               h[:, 4 * g + m, META + P * c:META + P * (c + 1)], ident)
                last.then_inc(s("out_t"), 1)

    @block.scalar
    def _(act):
        def copy(dst, src, scale=1.0):
            return nc.scalar.activation(dst, src, ACT.Copy, scale=scale)

        act.dma_start(square[:, :, :], dram["t_square"]).then_inc(s("square_loaded"), 16)
        act.dma_start(m_tok[:, 0, :], dram["meta_tokens"]).then_inc(s("m_loaded"), 16)
        act.dma_start(m_tok[:, 1, :], dram["meta_tokens_2"]).then_inc(s("m_loaded"), 16)
        for c in range(NFULL):
            act.dma_start(x_tok[:, c, :], dram["x"][0, P * c:P * (c + 1), :]).then_inc(s(f"x_loaded{c}"), 16)
        act_hi(act, 0, 0, 1, KT)
        act.wait_ge(s("rows_taken"), 1)
        for m in range(KT):
            act_x(act, 0, m, m, ROW_FOX, ("h_init", 9))

        def start(ph, body, r):
            body(0, lambda: act_rstd(act, r))
            loop(act, ph.n, body, 1)

        def plain(ph, r=None):
            def body(i, norm=None):
                for uj in range(ph.upi):
                    split_ahead(act, act_hi, ph, i, uj)
                    if norm and uj == 0:
                        norm()
            if r is None:
                loop(act, ph.n, body)
            else:
                start(ph, body, r)

        def sigmoid_tiles(ph, tile, done):
            tables_for(act, "sigmoid")
            def body(i):
                for uj in range(4):
                    split_ahead(act, act_hi, ph, i, uj)
                    act.wait_ge(s("psum_free"), evacuated(ph, i, uj))
                    t = tile(4 * i + uj)
                    carry(act, "act_carry")
                    nc.scalar.activation(t, t, ACT.Sigmoid).then_inc(s(done), 1)
            loop(act, ph.n, body)

        def residual(ph, r, gain_row):
            per = ph.upi // 4

            def body(i):
                for mm in range(4):
                    for n in range(per):
                        split_ahead(act, act_hi, ph, i, per * mm + n)
                    act_x(act, r, 4 * i + mm, mm, gain_row, ("psum_free", evacuated(ph, i, mm)))
            loop(act, ph.n, body)

        def up(n, ph, r):
            _, pre, t1, _, _ = ffn[n]
            cw = conv[:, n, :] if n < 2 else None

            def body(i, last=False):
                for mm in range(2):
                    m = 2 * i + mm
                    split_ahead(act, act_hi, ph, i, 2 * mm + 1)
                    act.wait_ge(s("psum_free"), evacuated(ph, i, 2 * mm))
                    carry(act, "act_carry")
                    if n < 2:
                        nc.scalar.activation(t1[:, mm, :], pre[:, mm, 2:L + 2], ACT.Identity,
                                             bias=col(cw, m + 3 * FT), scale=col(cw, m + 2 * FT)).then_inc(s("conv_a"), 1)
                        act.wait_ge(s("conv_c"), FT * n + 1 + m)
                        nc.scalar.activation(t1[:, mm, :], t1[:, mm, :], ACT.Silu).then_inc(s("silu"), 1)
                    else:
                        nc.scalar.activation(t1[:, mm, :], pre[:, mm, 2:L + 2], ACT.Silu).then_inc(s("silu"), 1)
                    if mm == 0:
                        split_ahead(act, act_hi, ph, i, 2)
                    elif not last:
                        split_ahead(act, act_hi, ph, i + 1, 0)
                    act.wait_ge(s("hid"), FT * n + 1 + m)
                    carry(act, "act_carry")
                    copy(row(ffn[n][0][0], m), t1[:, mm, :]).then_inc(s("hid_hi"), 1)
            split_ahead(act, act_hi, ph, 0, 0)
            act_rstd(act, r)
            tables_for(act, "silu")
            loop(act, ph.n - 1, body)
            body(ph.n - 1, True)

        plain(PH_QK, 0)
        act.wait_ge(s("lb_shifted"), 1)
        nc.scalar.activation(lb[:, 1:3, :], lb[:, 1:3, :], ACT.Exp).then_inc(s("lb_exp"), 1)
        act.wait_ge(s("psum_free"), PH_V.g0 + 2)

        def values(i):
            for uj in range(4):
                m = 4 * i + uj
                for j in range(2):
                    nc.scalar.activation(sq[:, j, :], row(heads, m + 8 * j), ACT.Square).then_inc(s("qn_sq"), 1)
                split_ahead(act, act_hi, PH_V, i, uj)
                for j in range(2):
                    act.wait_ge(s("qn_sum"), 2 * m + j + 1)
                    act.wait_ge(s("qn_done"), 2 * m + j + 1)
                    rt_j = two(post_t[:, j, :])
                    act_rsqrt(act, pair(4 + 2 * j), rt_j, rt_j, eps, "qn_ln", 2 * m + j).then_inc(s("qn_r"), 1)
        loop(act, PH_V.n, values)
        split_ahead(act, act_hi, PH_FOXF, 0, 0)
        act.wait_ge(s("fx_neg"), 1)
        nc.scalar.activation(fx[:, 2, :], fx[:, 1, :], ACT.Exp).then_inc(s("fx_exp"), 1)
        act.wait_ge(s("fx_exp"), 1)
        nc.scalar.activation(fx[:, 2, :], fx[:, 2, :], ACT.Ln, bias=one[0:FOX_H]).then_inc(s("fx_ln"), 1)
        sigmoid_tiles(PH_GATE, lambda m: row(heads, m + 24), "gate_ready")

        tables_for(act, "ln_exp")

        def pair_(i):
            copy(v_s[:, :], row(heads, i + 16)).then_inc(s("v_staged"), 1)

            def exps(b, tiles):
                for n in tiles:
                    w, k = TOK[n], P * n + TOK[n]
                    act.wait_ge(s("t_min"), 10 * i + 5 * b + ORDER.index(n) + 1)
                    tr = t_rows[0:w, b, ROWS0[n]:ROWS0[n] + k]
                    nc.scalar.activation(tr, tr, ACT.Exp, scale=-1.0, bias=rowmin[0:w, 5 * b + n:5 * b + n + 1],
                                         accum_out=rowsum[0:w, 5 * b + n:5 * b + n + 1]).then_inc(s("p_exp"), 1)
            exps(0, ORDER)
            exps(1, ORDER[:3])
            act.wait_ge(s("vt_mm"), i + 1)
            copy(v_t[:, 0:NFULL, :], ps[:, 4, :].rearrange("p (j n) -> p j n", j=NFULL))
            copy(v_t[0:TAIL, NFULL, :], ps[0:TAIL, 5, 0:P]).then_inc(s("vt_ready"), 1)
            exps(1, ORDER[3:])
            for b in range(2):
                act.wait_ge(s("pt_mm"), 2 * i + b + 1)
                copy(p_t[:, 0:512], ps[:, 4, :])
                copy(p_t[:, STRIP_C:tail_at(4)], ps[:, 6, 0:tail_at(4) - STRIP_C])
                copy(p_t[0:TAIL, tail_at(4):N_STRIP], ps[0:TAIL, 6, tail_at(4) - STRIP_C:N_STRIP - STRIP_C])\
                    .then_inc(s("pt_a"), 1)
            act.wait_ge(s("o_done"), i + 2)
            carry(act, "act_carry")
            copy(row(yh, i), o_t[:, :]).then_inc(s("yh_ready"), 1)
        loop(act, FOX_H // 2, pair_)
        residual(PH_FOXOUT, 1, ROW_FFN)
        up(0, PH_UP0, 1)
        residual(PH_DOWN0, 2, ROW_HGRN)

        def project(i, norm=None):
            for uj in range(4):
                split_ahead(act, act_hi, PH_HGRN, i, uj)
                if norm and uj == 0:
                    norm()
                    tables_for(act, "sigmoid")
                if uj == 3:
                    act.wait_ge(s("g_f_ready"), i + 1)
                    act.wait_ge(s("g_b_ready"), i + 1)
                    carry(act, "act_carry")
                    nc.scalar.activation(g_lf[:, :], row(heads, 4 * i + 1), ACT.Ln).then_inc(s("g_lf_ready"), 1)
                act.wait_ge(s("psum_free"), evacuated(PH_HGRN, i, uj))
                carry(act, "act_carry")
                t = row(heads, 4 * i + uj)
                if uj == 0:
                    nc.scalar.activation(sq[:, 0, :], t, ACT.Sigmoid).then_inc(s("g_sig"), 1)
                elif uj != 2:
                    nc.scalar.activation(t, t, ACT.Sigmoid).then_inc(s("g_gates"), 1)
        start(PH_HGRN, project, 2)
        tables_for(act, "ln_exp")

        def hgrn_square(i):
            act.wait_ge(s("g_o_ready"), i + 1)
            nc.scalar.activation(sq[:, 0, :], g_o[:, :], ACT.Square).then_inc(s("g_o_sq"), 1)

        def hgrn_rsqrt(i):
            act.wait_ge(s("g_o_sum"), i + 1)
            act_rsqrt(act, pair(4), two(g_r[:, :]), two(g_r[:, :]), eps, "g_ln", i).then_inc(s("g_r_ready"), 1)

        def hgrn_hi(i):
            act.wait_ge(s("g_out"), i + 1)
            carry(act, "act_carry")
            copy(row(yh, i), g_o[:, :]).then_inc(s("yh_ready"), 1)

        def hgrn(i):
            copy(g_q[:, :], row(heads, 4 * i))
            copy(g_v, row(heads, 4 * i + 2)).then_inc(s("g_staged"), 1)
            for n in range(HG_LEVELS):
                w = HG_LEVELS - 1 - n
                width, cols_ = 1 << w, (L if w <= 3 else SEQ)
                if n == 0:
                    act.wait_ge(s("g_d0_ready"), i + 1)
                else:
                    act.wait_ge(s("g_d_ready"), (HG_LEVELS - 1) * i + n)
                if n >= 2:
                    act.wait_ge(s("g_qk_ready"), HG_LEVELS * i + n - 1)
                d, e = (t[:, n % 2, 0:cols_].rearrange("p (b t) -> p b t", t=2 * width) for t in (g_d, g_e))
                nc.scalar.activation(e[:, :, width:], d[:, :, width:], ACT.Exp)
                nc.scalar.activation(e[:, :, 0:width], d[:, :, 0:width], ACT.Exp, scale=-1.0).then_inc(s("g_e_ready"), 1)
                if n == 0:
                    nc.scalar.activation(g_f[:, P:L], g_b[:, P:L], ACT.Exp)
                    for c in range(NFULL):
                        nc.scalar.activation(g_lf[:, P * c:P * (c + 1)], g_b[:, P * c:P * (c + 1)], ACT.Exp,
                                             scale=-1.0, bias=g_b[:, P * c + P - 1:P * (c + 1)])
                    nc.scalar.activation(exp_tot, g_b[:, 0:SEQ].rearrange("p (c t) -> p c t", t=P)[:, :, P - 1],
                                         ACT.Exp).then_inc(s("g_x_ready"), 1)
                if n == 1:
                    act.wait_ge(s("g_vt_mm"), i + 1)
                    copy(g_vt[:, 0:NFULL, :], ps[:, 4, :].rearrange("p (j n) -> p j n", j=NFULL))
                    copy(g_vt[0:TAIL, NFULL, :], ps[0:TAIL, 5, 0:P]).then_inc(s("g_vt_ready"), 1)
                    if not isinstance(i, int):
                        hgrn_square(i - 1)
            if not isinstance(i, int):
                hgrn_rsqrt(i - 1)
            act.wait_ge(s("g_off_mm"), i + 1)
            for c0, c1 in ((P, 512), (STRIP_B + P, STRIP_B + 3 * P), (STRIP_C + P, tail_at(4))):
                last = copy(g_off[:, c0:c1], flat[:, 2048 + c0:2048 + c1])
            last.then_inc(s("g_off_ready"), 1)
            if not isinstance(i, int):
                hgrn_hi(i - 1)
        hgrn(0)
        loop(act, HG_H, hgrn, 1)
        hgrn_square(HG_H - 1)
        hgrn_rsqrt(HG_H - 1)
        hgrn_hi(HG_H - 1)
        residual(PH_HGOUT, 3, ROW_FFN + KT)
        up(1, PH_UP1, 3)
        residual(PH_DOWN1, 4, ROW_MIXPRE)

        def ret(i, norm=None):
            def split(uj):
                split_ahead(act, act_hi, PH_RET, i, uj)

            def gate(uj):
                act.wait_ge(s("psum_free"), evacuated(PH_RET, i, uj))
                nc.scalar.activation(rt[:, uj, :], rt[:, uj, :], ACT.Silu).then_inc(s("r_g"), 1)

            for uj in range(8):
                split(uj)
                if norm and uj == 0:
                    norm()
            act.wait_ge(s("r_vt_mm"), 2 * i + 1)
            copy(r_vt[:, 0:NFULL, :], ps[:, 4:8, :]).then_inc(s("r_vt_ready"), 1)
            act.wait_ge(s("r_vt_mm"), 2 * i + 2)
            copy(r_vt[0:TAIL, NFULL, :], ps[0:TAIL, 7, :]).then_inc(s("r_vt_ready"), 1)
            split(8)
            act.wait_ge(s("r_y_mm"), 2 * i + 1)
            copy(r_y[:, :, 0:SEQ], ps[:, 4:8, :]).then_inc(s("r_y_ready"), 1)
            act.wait_ge(s("r_y_mm"), 2 * i + 2)
            copy(r_y[:, :, SEQ:L], ps[:, 4, 0:4 * TAIL].rearrange("p (e t) -> p e t", e=4)).then_inc(s("r_y_ready"), 1)
            split(9)
            gate(8)
            for e in range(4):
                act.wait_ge(s("r_cent"), 4 * i + e + 1)
                act.wait_ge(s("r_sq_used"), 4 * i + e + 1)
                nc.scalar.activation(sq[:, e % 2, :], r_y[:, e, :], ACT.Square).then_inc(s("r_sq"), 1)
            split(10)
            gate(9)
            split(11)
            gate(10)
            tables_for(act, "ln_exp")
            act.wait_ge(s("r_var_mm"), i + 1)
            act_rsqrt(act, pair(5), two(lnt[:, :]), two(r_t[:, 0, :]), gn_eps, "r_ln", i).then_inc(s("r_r"), 1)
            tables_for(act, "silu")
            gate(11)
            for e in range(4):
                act.wait_ge(s("r_out"), 4 * i + e + 1)
                copy(rh[:, e, :], r_y[:, e, :]).then_inc(s("r_out_hi"), 1)
            for m in range(KT):
                split(12 + m)
        start(PH_RET, ret, 4)
        tables_for(act, "sigmoid")

        def ga(i):
            for uj in range(4):
                split_ahead(act, act_hi, PH_GA, i, uj)
                act.wait_ge(s("psum_free"), evacuated(PH_GA, i, uj))
                nc.scalar.activation(sq[:, uj % 2, :], sq[:, uj % 2, :], ACT.Sigmoid).then_inc(s("ga_sig"), 1)
        loop(act, 2, ga)

        plain(PH_SB)
        sigmoid_tiles(PH_GB, lambda m: row(gb, m), "gb_ready")
        tables_for(act, "ln_exp")

        def sb_out(i):
            act.wait_ge(s("sb_o_mm"), 2 * i + 4)
            carry(act, "act_carry")
            copy(row(xh, i)[:, 0:SEQ], ps[:, 6, :])
            copy(row(xh, i)[:, SEQ:L], ps[:, 7, P:P + TAIL]).then_inc(s("sb_o_hi"), 1)

        def sb_pair(i):
            copy(s_v[:, :], row(sb, i + 16)).then_inc(s("sb_v"), 1)

            def softplus(b):
                act.wait_ge(s("sb_z"), 2 * i + b + 1)
                act.wait_ge(s("sb_sp"), 2 * i + b + 1)
                for c0, c1 in BANKS:
                    nc.scalar.activation(s_e[:, c0:c1], flat[:, 1536 * b + c0:1536 * b + c1], ACT.Abs)\
                        .then_inc(s("sb_abs"), 1)
                act.wait_ge(s("sb_abs"), 6 * i + 3 * b + 3)
                nc.scalar.activation(s_e[:, :], s_e[:, :], ACT.Exp, scale=-1.0).then_inc(s("sb_exp1"), 1)
                act.wait_ge(s("sb_exp1"), 2 * i + b + 1)
                nc.scalar.activation(s_e[:, :], s_e[:, :], ACT.Ln, bias=one).then_inc(s("sb_ln"), 1)

            def weights(b):
                act.wait_ge(s("sb_acc"), 2 * i + b + 3)
                act.wait_ge(s("sb_o_mm"), 2 * i + b + 1)
                for c0, c1 in BANKS:
                    last = nc.scalar.activation(s_a[:, b, c0:c1], flat[:, 1536 * b + c0:1536 * b + c1], ACT.Exp)
                last.then_inc(s("sb_a"), 1)
            softplus(0)
            if not isinstance(i, int):
                sb_out(i - 1)
            softplus(1)
            act.wait_ge(s("sb_vt_mm"), i + 1)
            copy(s_vt[:, 0:NFULL, :], ps[:, 6, :].rearrange("p (j n) -> p j n", j=NFULL))
            copy(s_vt[0:TAIL, NFULL, :], ps[0:TAIL, 7, 0:P]).then_inc(s("sb_vt_ready"), 1)
            weights(0)
            weights(1)
        sb_pair(0)
        loop(act, FOX_H // 2, sb_pair, 1)
        sb_out(FOX_H // 2 - 1)

        def merge(i):
            for uj in range(4):
                split_ahead(act, act_hi, PH_SBOUT, i, uj)
                act.wait_ge(s("merged"), 4 * i + uj + 1)
                carry(act, "act_carry")
                copy(row(mh, 4 * i + uj), m_t[:, uj % 2, :]).then_inc(s("m_hi"), 1)
        loop(act, 2, merge)

        def mixed(i):
            for uj in range(4):
                split_ahead(act, act_hi, PH_OUT, i, uj)
                act.wait_ge(s("psum_free"), evacuated(PH_OUT, i, uj))
                act_square(act, 5, 4 * i + uj, uj, row(mix, 4 * i + uj))
        for i in range(2):
            mixed(i)
        act_rstd(act, 5)
        for m in range(KT):
            act_x(act, 6, m, m, ROW_FFNPRE, ("h_post", m + 1))
        up(2, PH_UP2, 6)
        for i in range(2):
            for mm in range(4):
                for n in range(3):
                    split_ahead(act, act_hi, PH_DOWN2, i, 3 * mm + n, i == 1)
                act.wait_ge(s("psum_free"), evacuated(PH_DOWN2, i, mm))
                act_square(act, 7, 4 * i + mm, mm, ffn[2][4][:, 4 * i + mm, :])
        act_rstd(act, 7)

    @block.gpsimd
    def _(pool):
        pool_ssq(pool, 0)
        pool.wait_ge(s("c_ready"), 1)
        pool.dma_start(scratch, fx[:, 0, :]).then_inc(s("c_stored"), 16)
        pool.wait_ge(s("c_stored"), 16)

        def crep_(i):
            for b in range(2):
                pool.wait_ge(s("p_norm"), 2 * i + b + 1)
                pool.dma_start(crep[:, b, :], scratch[bass.ds(2 * i + b, 1), :].to_broadcast([P, L]))\
                    .then_inc(s(f"crep_loaded{b}"), 16)
        loop(pool, FOX_H // 2, crep_)
        pool_ssq(pool, 1)
        pool_ssq(pool, 2)
        pool.dma_start(restart[:, :], dram["t_restart"]).then_inc(s("restart_loaded"), 16)
        pool.dma_start(masks_f[:, :, :], dram["t_masks"]).then_inc(s("masks_loaded"), 16)

        def hgrn(i):
            for n in range(1, HG_LEVELS):
                if n == 1:
                    pool.wait_ge(s("g_b_staged"), 2 * i + 2)
                else:
                    pool.wait_ge(s("g_e_ready"), HG_LEVELS * i + n - 1)
                hgrn_distance(nc.gpsimd, n).then_inc(s("g_d_ready"), 1)
        loop(pool, HG_H, hgrn)
        pool_ssq(pool, 3)
        pool_ssq(pool, 4)
        nc.gpsimd.memset(yr[:, :, :], 0.0).then_inc(s("yr_zero"), 1)
        pool.dma_start(rotary[:, :, :], dram["t_rotary"]).then_inc(s("rotary_loaded"), 16)

        def ret(i):
            pool.wait_ge(s("r_s_ready"), i + 1)
            pool.dma_start(decay[:, :], dram["t_decay"][:, bass.ds(i, 1), :].rearrange("p a n -> p (a n)"))\
                .then_inc(s("decay_loaded"), 16)
            pool.wait_ge(s("r_y_ready"), 2 * i + 2)
            nc.gpsimd.tensor_tensor(r_sum[:, :], r_y[:, 0, :], r_y[:, 1, :], ALU.add).then_inc(s("r_adds"), 1)
            for e in range(2, 4):
                pool.wait_ge(s("r_adds"), 2 * i + e - 1)
                last = nc.gpsimd.tensor_tensor(r_sum[:, :], r_sum[:, :], r_y[:, e, :], ALU.add)
                last.then_inc(s("r_adds") if e == 2 else s("r_sum_ready"), 1)
            pool.wait_ge(s("r_mu_mm"), i + 1)
            for e in range(4):
                pool.wait_ge(s("r_sq"), 4 * i + e + 1)
                if e:
                    pool.wait_ge(s("r_sq_used"), 4 * i + e + 2)
                    nc.gpsimd.tensor_tensor(r_sum[:, :], r_sum[:, :], sq[:, e % 2, :], ALU.add).then_inc(s("r_sq_used"), 1)
                else:
                    carry(pool, "pool_carry")
                    nc.gpsimd.tensor_copy(r_sum[:, :], sq[:, 0, :]).then_inc(s("r_sq_used"), 1)
            pool.wait_ge(s("r_sq_used"), 4 * i + 6)
            pool.sem_inc(s("r_sum_ready"), 1)
        loop(pool, RET_H, ret)
        def sb_pair(i):
            def keep_earlier(t):
                for j in range(NTT):
                    at = STRIP0[j] if j < NFULL else tail_at(j)
                    blk = t[:, at:at + TOK[j]]
                    last = nc.gpsimd.affine_select(out=blk, in_=blk, compare_op=ALU.is_gt, fill=0.0, base=0,
                                                   pattern=[[1, TOK[j]]], channel_multiplier=-1)
                return last
            for b in range(2):
                pool.wait_ge(s("sb_sp"), 2 * i + b + 2)
                carry(pool, "pool_carry")
                keep_earlier(s_sp[:, b, :]).then_inc(s("sb_spm"), 1)
                pool.wait_ge(s("sb_a"), 2 * i + b + 1)
                carry(pool, "pool_carry")
                keep_earlier(s_a[:, b, :]).then_inc(s("sb_am"), 1)
        loop(pool, FOX_H // 2, sb_pair)
        pool_ssq(pool, 5)
        pool_ssq(pool, 6)
        pool_ssq(pool, 7)

    @block.vector
    def _(dve):
        V = nc.vector
        for name, n in (("w_split", RAW_SLOTS), ("mm_done", 2), ("psum_free", 2), ("sq_used", 2), ("qn_done", 2),
                        ("p_norm", 2), ("o_done", 1), ("r_s_ready", 1), ("r_sq_used", 2), ("sb_o_done", 1),
                        ("g_b_ready", 1), ("sb_acc", 2), ("sb_o_mm", 2), ("sb_sp", 1)):
            dve.sem_inc(s(name), n)

        def own(ins):
            own.n += 1
            ins.then_inc(s("setup"), 1)
            dve.wait_ge(s("setup"), own.n)
        own.n = 0

        V.memset(eps, EPS)
        V.memset(gn_eps, GN_EPS)
        V.memset(one, 1.0)
        V.memset(rowsum, 1.0)
        dve.wait_ge(s("x_t"), 1)
        V.tensor_copy(meta2[:, :, :], ps[:, 3, P:2 * P].rearrange("p (m t) -> p m t", m=KT))
        V.tensor_copy(h[:, :, 0:META], ps[:, 3, 0:P].rearrange("p (m t) -> p m t", m=KT)).then_inc(s("h_init"), 1)
        for c in range(NFULL):
            for g in range(2):
                b = 2 * c + g
                dve.wait_ge(s("x_t"), b + 2)
                V.tensor_copy(h[:, 4 * g:4 * g + 4, META + P * c:META + P * (c + 1)],
                              ps[:, 4 + b % 4, :].rearrange("p (m t) -> p m t", m=4)).then_inc(s("h_init"), 1)
        dve.wait_ge(s("rows_t"), 1)
        V.tensor_copy(conv[:, :, :], ps[:, 1:3, 0:4 * FT])
        own(V.tensor_copy(gains[:, :], ps[:, 0, 0:N_ROWS]))
        dve.sem_inc(s("rows_taken"), 1)
        dve_lo(dve, 0, 0, 1, KT)
        for m in range(KT):
            dve_x(dve, 0, m, ROW_FOX)
        own(V.tensor_scalar(gains[:, ROW_QGAIN:ROW_QGAIN + 1], gains[:, ROW_QGAIN:ROW_QGAIN + 1], -(FOX_D ** -0.5), None, ALU.mult))

        def scaled_out(ph, i, gj, dst):
            dve.wait_ge(s("mm_done"), group_end(ph, i, gj))
            return V.tensor_tensor(dst, out_pair(ph.g0 + gj), two(rstd[:, :]), ALU.mult).then_inc(s("psum_free"), 1)

        def store_tiles(ph, r, dst):
            def body(i):
                for uj in range(4):
                    split_ahead(dve, dve_lo, ph, i, uj)
                    dve.wait_ge(s("rstd_ready"), r + 1)
                    scaled_out(ph, i, uj, dst(4 * i + uj))
            loop(dve, ph.n, body)

        def residual(ph, rx, gain_row, skip=0):
            per = ph.upi // 4

            def body(i):
                for mm in range(4):
                    for n in range(per):
                        split_ahead(dve, dve_lo, ph, i, per * mm + n)
                    dve_add_h(dve, ph, i, mm, skip)
                    dve_x(dve, rx, 4 * i + mm, gain_row)
            loop(dve, ph.n, body)

        def up(n, ph, r):
            (hid_h, hid_l), pre, t1, t2, _ = ffn[n]
            cw = conv[:, n, :] if n < 2 else None
            if n < 2:
                own(V.memset(pre[:, :, 0:2], 0.0))

            def body(i, last=False):
                for mm in range(2):
                    m = 2 * i + mm
                    dve.wait_ge(s("rstd_ready"), r + 1)
                    scaled_out(ph, i, 2 * mm, two(pre[:, mm, 2:L + 2]))
                    split_ahead(dve, dve_lo, ph, i, 2 * mm + 1)
                    if n < 2:
                        dve.wait_ge(s("conv_a"), FT * n + 1 + m)
                        V.scalar_tensor_tensor(t2[:, :], pre[:, mm, 1:L + 1], col(cw, m + FT), t1[:, mm, :],
                                               ALU.mult, ALU.add).then_inc(s("conv_b"), 1)
                        dve.wait_ge(s("conv_b"), FT * n + 1 + m)
                        V.scalar_tensor_tensor(t1[:, mm, :], pre[:, mm, 0:L], col(cw, m), t2[:, :],
                                               ALU.mult, ALU.add).then_inc(s("conv_c"), 1)
                    if n < 2:
                        dve.wait_ge(s("conv_c"), FT * n + 1 + m)
                    scaled_out(ph, i, 2 * mm + 1, two(t2[:, :]))
                    dve.wait_ge(s("psum_free"), evacuated(ph, i, 2 * mm + 1))
                    dve.wait_ge(s("silu"), FT * n + 1 + m)
                    V.tensor_tensor(t1[:, mm, :], t1[:, mm, :], t2[:, :], ALU.mult).then_inc(s("hid"), 1)
                    if mm == 0:
                        split_ahead(dve, dve_lo, ph, i, 2)
                    elif not last:
                        split_ahead(dve, dve_lo, ph, i + 1, 0)
                    dve.wait_ge(s("hid_hi"), FT * n + 1 + m)
                    V.tensor_tensor(row(hid_l, m), t1[:, mm, :], row(hid_h, m).bitcast(F32), ALU.subtract)\
                        .then_inc(s("hid_ready"), 1)
            split_ahead(dve, dve_lo, ph, 0, 0)
            loop(dve, ph.n - 1, body)
            body(ph.n - 1, True)

        store_tiles(PH_QK, 0, lambda m: halves(heads, m))
        l0, l1 = gains[:, ROW_LB:ROW_LB + 8], gains[:, ROW_LB + 8:ROW_LB + 16]
        own(V.tensor_tensor(lb[:, 0, :], l0, l1, ALU.max))
        V.tensor_tensor(lb[:, 1, :], l0, lb[:, 0, :], ALU.subtract)
        V.tensor_tensor(lb[:, 2, :], l1, lb[:, 0, :], ALU.subtract).then_inc(s("lb_shifted"), 1)
        dve.wait_ge(s("lb_exp"), 1)
        own(V.tensor_tensor(lb[:, 3, :], lb[:, 1, :], lb[:, 2, :], ALU.add))
        own(V.reciprocal(lb[:, 3, :], lb[:, 3, :]))
        own(V.tensor_tensor(lb[:, 1, :], lb[:, 1, :], lb[:, 3, :], ALU.mult))
        own(V.tensor_tensor(lb[:, 2, :], lb[:, 2, :], lb[:, 3, :], ALU.mult))
        own(V.tensor_tensor(lb[:, 4, :], lb[:, 1, :], lb[:, 2, :], ALU.add))
        own(V.tensor_tensor(floor, lb[:, 4, :], lb[:, 1, :], ALU.subtract))
        own(V.tensor_scalar(span, floor, -1.0, 1.0, ALU.mult, ALU.add))

        def values(i):
            for uj in range(4):
                m = 4 * i + uj
                split_ahead(dve, dve_lo, PH_V, i, uj)
                for j in range(2):
                    dve.wait_ge(s("qn_r"), 2 * m + j + 1)
                    V.scalar_tensor_tensor(row(heads, m + 8 * j), row(heads, m + 8 * j),
                                           gains[:, ROW_QGAIN + j:ROW_QGAIN + j + 1], post_t[:, j, :],
                                           ALU.mult, ALU.mult).then_inc(s("qn_done"), 1)
                scaled_out(PH_V, i, uj, halves(heads, m + 16))
        loop(dve, PH_V.n, values)
        split_ahead(dve, dve_lo, PH_FOXF, 0, 0)
        dve.wait_ge(s("mm_done"), group_end(PH_FOXF, 0, 0))
        V.tensor_tensor(two(fx[:, 0, :]), out_pair(PH_FOXF.g0)[0:FOX_H], two(rstd[0:FOX_H, :]), ALU.mult)\
            .then_inc(s("psum_free"), 1)
        dve.wait_ge(s("psum_free"), evacuated(PH_FOXF, 0, 0))
        own(V.tensor_scalar(fx[:, 0, :], fx[:, 0, :], bf, None, ALU.add))
        V.scalar_tensor_tensor(fx[:, 1, :], fx[:, 0, :], -1.0, fx[:, 0, :], ALU.mult, ALU.min).then_inc(s("fx_neg"), 1)
        own(V.memset(fx[:, 3, :], 1.0))
        dve.wait_ge(s("fx_ln"), 1)
        own(V.scalar_tensor_tensor(fx[:, 1, :], fx[:, 0, :], 0.0, fx[:, 2, :], ALU.min, ALU.subtract))
        V.tensor_tensor_scan(fx[:, 0, :], fx[:, 3, :], fx[:, 1, :], 0.0, ALU.mult, ALU.add).then_inc(s("c_ready"), 1)
        store_tiles(PH_GATE, 0, lambda m: halves(heads, m + 24))

        dve.wait_ge(s("qn_done"), 2 * KT + 2)
        dve.wait_ge(s("gate_ready"), KT)

        def pair_(i):
            V.tensor_copy(q_s[:, :], row(heads, i)).then_inc(s("qk_staged"), 1)
            V.tensor_copy(k_s[:, :], row(heads, i + 8)).then_inc(s("qk_staged"), 1)

            def least(b, turns):
                if 0 in turns:
                    dve.wait_ge(s(f"crep_loaded{b}"), 16 * i + 16)
                for turn in turns:
                    dve.wait_ge(s("s_done"), 6 * i + 3 * b + turn + 1)
                    carry(dve, "dve_carry")
                    for n in TURNS[turn]:
                        w, k = TOK[n], P * n + TOK[n]
                        V.tensor_tensor_reduce(out=t_rows[0:w, b, ROWS0[n]:ROWS0[n] + k],
                                               in0=flat[0:w, SCORES0[n]:SCORES0[n] + k], in1=crep[0:w, b, 0:k],
                                               scale=1.0, scalar=3e38, op0=ALU.add, op1=ALU.min,
                                               accum_out=rowmin[0:w, 5 * b + n:5 * b + n + 1]).then_inc(s("t_min"), 1)

            def normalise(b):
                dve.wait_ge(s("p_exp"), 10 * i + 5 * b + 5)
                V.reciprocal(rowinv[:, 5 * b:5 * b + 5], rowsum[:, 5 * b:5 * b + 5]).then_inc(s("p_inv"), 1)
                dve.wait_ge(s("p_inv"), 2 * i + b + 1)
                for n in range(NTT):
                    w, k = TOK[n], P * n + TOK[n]
                    tr = t_rows[0:w, b, ROWS0[n]:ROWS0[n] + k]
                    last = V.tensor_scalar(tr, tr, rowinv[0:w, 5 * b + n:5 * b + n + 1], None, ALU.mult)
                last.then_inc(s("p_norm"), 1)

            def evacuate(b):
                dve.wait_ge(s("pt_mm"), 2 * i + b + 1)
                V.tensor_copy(p_t[:, 512:1024], ps[:, 5, :]).then_inc(s("pt_b"), 1)
            least(0, range(3))
            least(1, range(2))
            normalise(0)
            least(1, [2])
            evacuate(0)
            normalise(1)
            evacuate(1)
            dve.wait_ge(s("o_mm"), 2 * i + 2)
            gate = row(heads, i + 24)
            V.tensor_tensor(o_t[:, 0:SEQ], ps[:, 7, :], gate[:, 0:SEQ], ALU.mult)
            V.tensor_tensor(o_t[:, SEQ:L], ps[:, 6, 496:512], gate[:, SEQ:L], ALU.mult).then_inc(s("o_done"), 1)
            dve.wait_ge(s("o_done"), i + 2)
            dve.wait_ge(s("yh_ready"), i + 1)
            V.tensor_tensor(row(yl, i), o_t[:, :], row(yh, i).bitcast(F32), ALU.subtract).then_inc(s("y_ready"), 1)
        loop(dve, FOX_H // 2, pair_)
        residual(PH_FOXOUT, 1, ROW_FFN)
        up(0, PH_UP0, 1)
        residual(PH_DOWN0, 2, ROW_HGRN)


        def project(i):
            for uj in range(4):
                split_ahead(dve, dve_lo, PH_HGRN, i, uj)
                dve.wait_ge(s("rstd_ready"), 3)
                if uj == 2:
                    f_row = row(heads, 4 * i + 1)
                    dve.wait_ge(s("g_gates"), 2 * i + 1)
                    V.tensor_scalar(f_row, f_row, col(span, i), col(floor, i), ALU.mult, ALU.add).then_inc(s("g_f_ready"), 1)
                    dve.wait_ge(s("g_f_ready"), i + 1)
                    V.tensor_scalar(row(yl, i).bitcast(F32), f_row, -1.0, 1.0, ALU.mult, ALU.add).then_inc(s("g_k_ready"), 1)
                if uj == 3:
                    dve.wait_ge(s("restart_loaded"), 16)
                    dve.wait_ge(s("g_k_ready"), i + 1)
                    dve.wait_ge(s("g_lf_ready"), i + 1)
                    V.tensor_tensor_scan(row(heads, 4 * i + 1), restart[:, :], g_lf[:, :], 0.0, ALU.mult, ALU.add)\
                        .then_inc(s("g_b_ready"), 1)
                scaled_out(PH_HGRN, i, uj, halves(heads, 4 * i + uj))
                if uj == 0:
                    dve.wait_ge(s("psum_free"), evacuated(PH_HGRN, i, 0))
                    dve.wait_ge(s("g_sig"), i + 1)
                    V.tensor_tensor(row(heads, 4 * i), row(heads, 4 * i), sq[:, 0, :], ALU.mult).then_inc(s("g_silu"), 1)
        loop(dve, HG_H, project)
        dve.wait_ge(s("g_gates"), 2 * HG_H)
        V.memset(g_diag[:, :], 0.0)
        V.memset(g_k[:, L:NTT * P], 0.0)
        dve.wait_ge(s("masks_loaded"), 16)
        V.tensor_copy(masks[:, :, :], masks_f[:, :, :])
        own(V.memset(g_qk[:, :, L:NTT * P], 0.0))

        def hgrn_out(i):
            dve.wait_ge(s("g_r_ready"), i + 1)
            V.scalar_tensor_tensor(g_o[:, :], g_o[:, :], gains[:, ROW_OGAIN:ROW_OGAIN + 1], g_r[:, :],
                                   ALU.mult, ALU.mult).then_inc(s("g_normed"), 1)
            dve.wait_ge(s("g_normed"), i + 1)
            V.tensor_tensor(g_o[:, :], g_o[:, :], row(heads, 4 * i + 3), ALU.mult).then_inc(s("g_out"), 1)
            dve.wait_ge(s("g_out"), i + 1)
            dve.wait_ge(s("yh_ready"), i + 9)
            V.tensor_tensor(row(yl, i), g_o[:, :], row(yh, i).bitcast(F32), ALU.subtract).then_inc(s("y_ready"), 1)

        def hgrn(i):
            V.tensor_copy(g_b[:, :], row(heads, 4 * i + 1)).then_inc(s("g_b_staged"), 1)
            V.tensor_copy(g_k[:, 0:L], row(yl, i).bitcast(F32)).then_inc(s("g_b_staged"), 1)
            dve.wait_ge(s("g_b_staged"), 2 * i + 2)
            hgrn_distance(V, 0).then_inc(s("g_d0_ready"), 1)
            dve.wait_ge(s("g_staged"), i + 1)

            def pick(n):
                cols_ = hgrn_level(n)[1] if n < HG_LEVELS else L
                dve.wait_ge(s("g_lv_mm"), (HG_LEVELS + 1) * i + n + 1)
                if n:
                    dve.wait_ge(s("g_lv_used"), (HG_LEVELS + 1) * i + n)
                carry(dve, "dve_carry")
                pr = 1024 * (n % 2)
                V.copy_predicated(g_diag[:, 0:cols_], masks[:, HG_LEVELS - 1 - n if n < HG_LEVELS else n, 0:cols_],
                                  flat[:, pr:pr + cols_]).then_inc(s("g_lv_used"), 1)

            for n in range(HG_LEVELS):
                width, cols_ = hgrn_level(n)
                dve.wait_ge(s("g_e_ready"), HG_LEVELS * i + n + 1)
                e, qk, q, k = (t.rearrange("p (b t) -> p b t", t=2 * width) for t in
                               (g_e[:, n % 2, 0:cols_], g_qk[:, n % 2, 0:cols_], g_q[:, 0:cols_], g_k[:, 0:cols_]))
                V.tensor_tensor(qk[:, :, width:], e[:, :, width:], q[:, :, width:], ALU.mult)
                V.tensor_tensor(qk[:, :, 0:width], e[:, :, 0:width], k[:, :, 0:width], ALU.mult)\
                    .then_inc(s("g_qk_ready"), 1)
                if n:
                    pick(n - 1)
                if n == 1:
                    dve.wait_ge(s("g_x_ready"), i + 1)
                    V.tensor_tensor(g_f[:, P:L], g_f[:, P:L], g_q[:, P:L], ALU.mult)
                    for c in range(NFULL):
                        last = V.tensor_tensor(g_left[:, c * (c + 3) // 2, :], g_lf[:, P * c:P * (c + 1)],
                                               g_k[:, P * c:P * (c + 1)], ALU.mult)
                    last.then_inc(s("g_left_step"), 1)
                    for j in range(2, NTT):
                        dve.wait_ge(s("g_left_step"), 3 * i + j - 1)
                        a0, a1, n_ = (j - 1) * (j - 2) // 2, j * (j - 1) // 2, j - 1
                        last = V.tensor_scalar(g_left[:, a1:a1 + n_, :], g_left[:, a0:a0 + n_, :],
                                               exp_tot[:, j - 1:j], None, ALU.mult)
                        last.then_inc(s("g_left_step") if j < NFULL else s("g_left_ready"), 1)
            pick(HG_LEVELS - 1)
            pick(HG_LEVELS)
            if not isinstance(i, int):
                hgrn_out(i - 1)
                dve.wait_ge(s("y_ready"), KT + i)
            dve.wait_ge(s("g_o_mm"), i + 1)
            V.tensor_copy(g_o[:, 0:SEQ], ps[:, 7, :])
            V.tensor_copy(g_o[:, SEQ:L], ps[:, 6, 496:512]).then_inc(s("g_o_ready"), 1)
        hgrn(0)
        loop(dve, HG_H, hgrn, 1)
        hgrn_out(HG_H - 1)
        residual(PH_HGOUT, 3, ROW_FFN + KT)
        up(1, PH_UP1, 3)
        own(V.tensor_copy(h[:, :, 0:META], meta2[:, :, :]))
        residual(PH_DOWN1, 4, ROW_MIXPRE, skip=META)

        def ret(i):
            def rotate(x1, x2, n):
                c, sn = rotary[:, 0, :], rotary[:, 1, :]
                if n:
                    dve.wait_ge(s("r_rot_add"), i + 1)
                V.tensor_tensor(r_t[:, 0, :], x1, sn, ALU.mult)
                V.tensor_tensor(r_t[:, 1, :], x2, sn, ALU.mult)
                V.tensor_tensor(x1, x1, c, ALU.mult)
                V.tensor_tensor(x2, x2, c, ALU.mult).then_inc(s("r_rot_mul"), 1)
                dve.wait_ge(s("r_rot_mul"), 2 * i + n + 1)
                V.tensor_tensor(x1, x1, r_t[:, 1, :], ALU.subtract)
                return V.tensor_tensor(x2, x2, r_t[:, 0, :], ALU.add)

            for uj in range(8):
                split_ahead(dve, dve_lo, PH_RET, i, uj)
                dve.wait_ge(s("rstd_ready"), 5)
                scaled_out(PH_RET, i, uj, two(rt[:, uj, :]))
                if uj == 4:
                    dve.wait_ge(s("psum_free"), evacuated(PH_RET, i, 4))
                    dve.wait_ge(s("rotary_loaded"), 16)
                    rotate(rt[:, 0, :], rt[:, 1, :], 0).then_inc(s("r_rot_add"), 1)
                if uj == 6:
                    rotate(rt[:, 2, :], rt[:, 3, :], 1).then_inc(s("r_rot"), 1)
            split_ahead(dve, dve_lo, PH_RET, i, 8)
            dve.wait_ge(s("r_s_mm"), i + 1)
            dve.wait_ge(s("decay_loaded"), 16 * i + 16)
            for c0, c1, k in ((0, 512, P), (512, 1024, P), (STRIP_C, tail_at(4), P), (tail_at(4), N_STRIP, TAIL)):
                last = V.tensor_tensor(r_s[0:k, c0:c1], flat[0:k, 2048 + c0:2048 + c1], decay[0:k, c0:c1], ALU.mult)
            last.then_inc(s("r_s_ready"), 1)
            scaled_out(PH_RET, i, 8, two(rt[:, 8, :]))
            split_ahead(dve, dve_lo, PH_RET, i, 9)
            dve.wait_ge(s("r_mu_mm"), i + 1)
            for e in range(4):
                V.tensor_tensor(two(r_y[:, e, :]), two(r_y[:, e, :]), pair(5), ALU.subtract).then_inc(s("r_cent"), 1)
            for uj in (9, 10):
                scaled_out(PH_RET, i, uj, two(rt[:, uj, :]))
                split_ahead(dve, dve_lo, PH_RET, i, uj + 1)
            dve.wait_ge(s("r_r"), i + 1)
            for e in range(4):
                V.tensor_tensor(r_y[:, e, :], r_y[:, e, :], lnt[:, :], ALU.mult).then_inc(s("r_normed"), 1)
            scaled_out(PH_RET, i, 11, two(rt[:, 11, :]))
            dve.wait_ge(s("r_g"), 4 * i + 4)
            for e in range(4):
                dve.wait_ge(s("r_normed"), 4 * i + e + 1)
                V.tensor_tensor(r_y[:, e, :], r_y[:, e, :], rt[:, 8 + e, :], ALU.mult).then_inc(s("r_out"), 1)
            for e in range(4):
                dve.wait_ge(s("r_out_hi"), 4 * i + e + 1)
                V.tensor_tensor(rl[:, e, :], r_y[:, e, :], rh[:, e, :].bitcast(F32), ALU.subtract)\
                    .then_inc(s("r_out_ready"), 1)
            dve.wait_ge(s("yr_zero"), 1)
            for m in range(KT):
                split_ahead(dve, dve_lo, PH_RET, i, 12 + m)
                dve.wait_ge(s("mm_done"), group_end(PH_RET, i, 12 + m))
                V.tensor_tensor(two(yr[:, m, :]), two(yr[:, m, :]), out_pair(PH_RET.g0 + m), ALU.add)\
                    .then_inc(s("psum_free"), 1)
        loop(dve, RET_H, ret)

        def ga(i):
            for uj in range(4):
                split_ahead(dve, dve_lo, PH_GA, i, uj)
                scaled_out(PH_GA, i, uj, two(sq[:, uj % 2, :]))
                dve.wait_ge(s("ga_sig"), 4 * i + uj + 1)
                V.tensor_tensor(row(yr, 4 * i + uj), row(yr, 4 * i + uj), sq[:, uj % 2, :], ALU.mult)\
                    .then_inc(s("ga_done"), 1)
        loop(dve, 2, ga)

        store_tiles(PH_SB, 4, lambda m: halves(sb, m))
        store_tiles(PH_GB, 4, lambda m: halves(gb, m))
        V.memset(s_k[:, L:NTT * P], 0.0)
        dve.wait_ge(s("gb_ready"), KT)

        def sb_stage(i):
            V.tensor_scalar(s_q[:, :], row(sb, i), SB_SCALE, None, ALU.mult).then_inc(s("sb_staged"), 1)
            V.tensor_copy(s_k[:, 0:L], row(sb, i + 8)).then_inc(s("sb_staged"), 1)

        def sb_out(i):
            dve.wait_ge(s("sb_o_mm"), 2 * i + 4)
            dve.wait_ge(s("sb_o_hi"), i + 1)
            V.tensor_tensor(row(xl, i)[:, 0:SEQ], ps[:, 6, :], row(xh, i)[:, 0:SEQ].bitcast(F32), ALU.subtract)
            V.tensor_tensor(row(xl, i)[:, SEQ:L], ps[:, 7, P:P + TAIL], row(xh, i)[:, SEQ:L].bitcast(F32), ALU.subtract)\
                .then_inc(s("sb_o_done"), 1)

        def sb_pair(i):
            for b in range(2):
                z = 1536 * b
                dve.wait_ge(s("sb_ln"), 2 * i + b + 1)
                dve.wait_ge(s("sb_acc"), 2 * i + b + 1)
                for c0, c1 in BANKS:
                    last = V.scalar_tensor_tensor(s_sp[:, b, c0:c1], flat[:, z + c0:z + c1], 0.0, s_e[:, c0:c1],
                                                  ALU.max, ALU.add)
                last.then_inc(s("sb_sp"), 1)
                if b == 0 and not isinstance(i, int):
                    sb_out(i - 1)
            sb_stage(i + 1)
        sb_stage(0)
        sb_pair(0)
        loop(dve, FOX_H // 2, sb_pair, 1)
        sb_out(FOX_H // 2 - 1)

        def merge(i):
            for uj in range(4):
                m = 4 * i + uj
                split_ahead(dve, dve_lo, PH_SBOUT, i, uj)
                dve.wait_ge(s("mm_done"), group_end(PH_SBOUT, i, uj))
                V.tensor_tensor(two(m_t[:, uj % 2, :]), out_pair(PH_SBOUT.g0 + uj), halves(gb, m), ALU.mult)\
                    .then_inc(s("psum_free"), 1)
                dve.wait_ge(s("psum_free"), evacuated(PH_SBOUT, i, uj))
                V.tensor_tensor(m_t[:, uj % 2, :], m_t[:, uj % 2, :], row(yr, m), ALU.add).then_inc(s("merged"), 1)
                dve.wait_ge(s("m_hi"), m + 1)
                V.tensor_tensor(row(ml, m), m_t[:, uj % 2, :], row(mh, m).bitcast(F32), ALU.subtract)\
                    .then_inc(s("m_ready"), 1)
        loop(dve, 2, merge)
        for i in range(2):
            for uj in range(4):
                split_ahead(dve, dve_lo, PH_OUT, i, uj)
                dve.wait_ge(s("mm_done"), group_end(PH_OUT, i, uj))
                V.tensor_copy(halves(mix, 4 * i + uj), out_pair(PH_OUT.g0 + uj)).then_inc(s("psum_free"), 1)
        post_norm(dve, mix, ROW_MIXPOST, 5, 0, "h_post", 5, ROW_FFNPRE)
        up(2, PH_UP2, 6)
        ff = ffn[2][4]
        for i in range(2):
            for mm in range(4):
                for n in range(3):
                    split_ahead(dve, dve_lo, PH_DOWN2, i, 3 * mm + n, i == 1)
                dve.wait_ge(s("mm_done"), group_end(PH_DOWN2, i, mm))
                V.tensor_copy(halves(ff, 4 * i + mm), out_pair(PH_DOWN2.g0 + mm)).then_inc(s("psum_free"), 1)
        post_norm(dve, ff, ROW_FFNPOST, 7, KT, "out_ready", None, None)
        for c in range(NFULL):
            for g in range(2):
                b = 2 * c + g
                dve.wait_ge(s("out_t"), b + 1)
                if c >= 2:
                    dve.wait_ge(s(f"stored{c % 2}"), 16)
                V.tensor_copy(o_tok[:, c % 2, 512 * g:512 * (g + 1)], ps[:, 4 + b % 4, :]).then_inc(s("o_tok_ready"), 1)


_INS = ["x", "meta_tokens", "fox_norm", "fox_w_in", "fox_b_f", "fox_q_gain", "fox_k_gain", "fox_w_out", "hgrn_norm",
        "hgrn_w_in", "hgrn_lower_bounds", "hgrn_o_gain", "hgrn_w_out", "ffn_norm", "ffn_w_gate", "ffn_w_up",
        "ffn_conv_w", "ffn_conv_b", "ffn_w_down", "meta_tokens_2", "w_in_2", "w_ret_out_2", "w_sb_out_2", "w_out_2",
        "w_ffn_in_2", "w_ffn_out_2", "norm_mix_pre_2", "norm_mix_post_2", "norm_ffn_pre_2", "norm_ffn_post_2"]


def kernel(**inputs):
    import concourse.bacc as bacc
    from concourse.bass_utils import run_bass_kernel_spmd

    nc = bacc.Bacc("TRN2", target_bir_lowering=False, num_devices=1)
    arrays, dram = {}, {}
    for name in _INS:
        arrays[f"in_{name}"] = np.ascontiguousarray(inputs[name])
    for name, table in tables().items():
        arrays[f"in_{name}"] = table
    for name, a in arrays.items():
        dram[name[3:]] = nc.dram_tensor(name, a.shape, mybir.dt.from_np(a.dtype), kind="ExternalInput").ap()
    out = nc.dram_tensor("out", (1, SEQ, D), F32, kind="ExternalOutput").ap()
    build(nc, dram, out)
    result = run_bass_kernel_spmd(nc, [arrays], core_ids=[0])
    return result.results[0]["out"]
```
